# Optimizing a Trainium2 kernel written in Bass

```python
import math
import jax, jax.numpy as jnp
from jax import lax
import numpy as np

D_MODEL = 1024
BATCH = 1
SEQ = 512
DEPTH = 1
DEC_BATCH = 1
DEC_SEQ = 256
PAST_LEN = 128

DIL_PAIRS = ((128, 1), (512, 4), (2048, 16))
N_DIL_GROUPS = 3
A_HEADS_PER_GROUP = 4
A_HEADS = N_DIL_GROUPS * A_HEADS_PER_GROUP
A_HEAD_DIM = 64
A_QKV = A_HEADS * A_HEAD_DIM
A_OUT = A_HEADS_PER_GROUP * A_HEAD_DIM
Q_BLOCK = 128
NEG_INF = -1e30
N_REL_BUCKETS = 32
REL_MAX_DISTANCE = 1024
GLA_HEADS = 4
GLA_K_WIDTH = D_MODEL // 2
GLA_V_WIDTH = D_MODEL
GLA_DK = GLA_K_WIDTH // GLA_HEADS
GLA_DV = GLA_V_WIDTH // GLA_HEADS
GATE_RANK = 16
GATE_TAU = 16.0
GLA_CHUNK = 64
N_GROUPS = 4
EXPERTS_PER_GROUP = 8
N_EXPERTS = N_GROUPS * EXPERTS_PER_GROUP
EXPERT_FF = 256
TOP_K_INNER = 2
EPS = 1e-6
SPLITS = (A_QKV, A_QKV, A_QKV, GLA_K_WIDTH, GLA_K_WIDTH, GLA_V_WIDTH, GLA_V_WIDTH, GATE_RANK, GATE_RANK, D_MODEL, D_MODEL)
IN_WIDTH = sum(SPLITS)

kernel_name = 'hybrid_dilated_gla_hmoe_encoder'

def rmsnorm(x, g):
    xf = x.astype(jnp.float32)
    r = xf * lax.rsqrt(jnp.mean(xf * xf, axis=-1, keepdims=True) + EPS)
    return (r * g.astype(jnp.float32)).astype(x.dtype)

def t5_buckets(rel):
    nb = N_REL_BUCKETS // 2
    max_exact = nb // 2
    ret = (rel > 0).astype(np.int64) * nb
    n = np.abs(rel)
    large = max_exact + (np.log(np.maximum(n, 1) / max_exact) / math.log(REL_MAX_DISTANCE / max_exact) * (nb - max_exact)).astype(np.int64)
    large = np.minimum(large, nb - 1)
    return (ret + np.where(n < max_exact, n, large)).astype(np.int32)

def dilated_group_attention(q, k, v, bias, rel):
    B, S, H, Dh = q.shape
    rel_j = jnp.asarray(rel, jnp.int32)
    nblk = S // Q_BLOCK
    q_blocks = q.reshape(B, nblk, Q_BLOCK, H, Dh).swapaxes(0, 1)
    scale = A_HEAD_DIM ** -0.5
    bias_f = bias.astype(jnp.float32)[None, :, None, :]

    def one_block(args):
        i, q_blk = args
        pos = i * Q_BLOCK + jnp.arange(Q_BLOCK, dtype=jnp.int32)
        kpos = pos[:, None] + rel_j[None, :]
        valid = (kpos >= 0) & (kpos < S)
        idx = jnp.clip(kpos, 0, S - 1)
        k_g = k[:, idx]
        v_g = v[:, idx]
        s = jnp.einsum('bqhd,bqjhd->bhqj', q_blk, k_g).astype(jnp.float32) * scale + bias_f
        s = jnp.where(valid[None, None], s, NEG_INF)
        lse = jax.nn.logsumexp(s, axis=-1)
        p = jnp.exp(s - lse[..., None])
        o = jnp.einsum('bhqj,bqjhd->bqhd', p.astype(v.dtype), v_g)
        return o, lse.swapaxes(1, 2)

    o, lse = lax.map(one_block, (jnp.arange(nblk, dtype=jnp.int32), q_blocks))
    o = o.swapaxes(0, 1).reshape(B, S, H, Dh)
    lse = lse.swapaxes(0, 1).reshape(B, S, H)
    return o, lse

def gla_chunked(q, k, v, logg, strict):
    B, S, H, dk = q.shape
    dv = v.shape[-1]
    n = S // GLA_CHUNK
    q, k, v, logg = [t.reshape(B, n, GLA_CHUNK, H, t.shape[-1]) for t in (q, k, v, logg)]
    b = jnp.cumsum(logg, axis=2)
    b_last = b[:, :, -1:]
    q_in = q * jnp.exp(b)
    k_in = k * jnp.exp(-b)
    k_out = k * jnp.exp(b_last - b)
    scores = jnp.einsum('bnihd,bnjhd->bnhij', q_in, k_in)
    mask = jnp.tril(jnp.ones((GLA_CHUNK, GLA_CHUNK), dtype=bool), -1 if strict else 0)
    scores = jnp.where(mask, scores, 0.0)
    o_intra = jnp.einsum('bnhij,bnjhv->bnihv', scores, v)

    def step(state, xs):
        q_c, k_c, v_c, decay_c = xs
        o_c = jnp.einsum('bihd,bhdv->bihv', q_c, state)
        state = decay_c[..., None] * state + jnp.einsum('bjhd,bjhv->bhdv', k_c, v_c)
        return state, o_c

    xs = (q_in.swapaxes(0, 1), k_out.swapaxes(0, 1), v.swapaxes(0, 1), jnp.exp(b_last[:, :, 0]).swapaxes(0, 1))
    state0 = jnp.zeros((B, H, dk, dv), jnp.float32)
    _, o_inter = lax.scan(step, state0, xs)
    return (o_intra + o_inter.swapaxes(0, 1)).reshape(B, S, H, dv)

def hier_moe(h, w_rg, b_rg, w_re, b_re, w_eg, w_eu, w_ed):
    T = h.shape[0]
    g_logits = (h @ w_rg + b_rg).astype(jnp.float32)
    pg = jax.nn.softmax(g_logits, axis=-1)
    pg_top, g_sel = lax.top_k(pg, 1)
    e_logits = (h @ w_re + b_re).astype(jnp.float32).reshape(T, N_GROUPS, EXPERTS_PER_GROUP)
    e_logits = jnp.take_along_axis(e_logits, g_sel[:, :, None], axis=1)[:, 0]
    pe = jax.nn.softmax(e_logits, axis=-1)
    pe_top, e_sel = lax.top_k(pe, TOP_K_INNER)
    pe_top = pe_top / jnp.sum(pe_top, axis=-1, keepdims=True)
    weights = pg_top * pe_top
    gidx = g_sel * EXPERTS_PER_GROUP + e_sel
    gate = jnp.sum(jax.nn.one_hot(gidx, N_EXPERTS, dtype=jnp.float32) * weights[..., None], axis=1).astype(h.dtype)
    out = jnp.zeros_like(h)
    for e in range(N_EXPERTS):
        a = jax.nn.silu(h @ w_eg[e]) * (h @ w_eu[e])
        out = out + gate[:, e:e + 1] * (a @ w_ed[e])
    return out

def encoder_layer(x, norm_mix, w_in, rel_bias, w_gate_f, b_gate_f, w_gate_b, b_gate_b, gla_norm,
                  w_proj_a, w_proj_b, w_out, norm_moe, w_rg, b_rg, w_re, b_re, w_eg, w_eu, w_ed):
    B, S, _ = x.shape
    dt = x.dtype
    h = rmsnorm(x, norm_mix)
    proj = h @ w_in
    split_points = np.cumsum(SPLITS)[:-1].tolist()
    qa, ka, va, qb, kb, vb, og, gf, gb, ma, mb = jnp.split(proj, split_points, axis=-1)

    qa = qa.reshape(B, S, A_HEADS, A_HEAD_DIM)
    ka = ka.reshape(B, S, A_HEADS, A_HEAD_DIM)
    va = va.reshape(B, S, A_HEADS, A_HEAD_DIM)
    outs, lses = [], []
    for g, (win, dil) in enumerate(DIL_PAIRS):
        half = win // (2 * dil)
        rel = dil * np.arange(-half, half + 1)
        bucket = jnp.asarray(t5_buckets(rel))
        hs = slice(g * A_HEADS_PER_GROUP, (g + 1) * A_HEADS_PER_GROUP)
        bias = rel_bias[bucket][:, hs].T
        o, l = dilated_group_attention(qa[:, :, hs], ka[:, :, hs], va[:, :, hs], bias, rel)
        outs.append(o)
        lses.append(l)
    w_grp = jax.nn.softmax(jnp.stack(lses), axis=0)
    oa = jnp.sum(w_grp[..., None].astype(dt) * jnp.stack(outs), axis=0)
    ya = oa.reshape(B, S, A_OUT) @ w_proj_a

    f32 = jnp.float32
    qb = qb.reshape(B, S, GLA_HEADS, GLA_DK).astype(f32) * (GLA_DK ** -0.5)
    kb = kb.reshape(B, S, GLA_HEADS, GLA_DK).astype(f32)
    vb = vb.reshape(B, S, GLA_HEADS, GLA_DV).astype(f32)
    logg_f = (jax.nn.log_sigmoid((gf @ w_gate_f + b_gate_f).astype(f32)) / GATE_TAU).reshape(B, S, GLA_HEADS, GLA_DK)
    logg_b = (jax.nn.log_sigmoid((gb @ w_gate_b + b_gate_b).astype(f32)) / GATE_TAU).reshape(B, S, GLA_HEADS, GLA_DK)
    o_f = gla_chunked(qb, kb, vb, logg_f, False)
    flip = lambda t: jnp.flip(t, axis=1)
    o_b = flip(gla_chunked(flip(qb), flip(kb), flip(vb), flip(logg_b), True))
    ob = rmsnorm(o_f + o_b, gla_norm).reshape(B, S, GLA_V_WIDTH).astype(dt) * jax.nn.silu(og)
    yb = ob @ w_proj_b

    mix = jax.nn.sigmoid(ma) * ya + jax.nn.sigmoid(mb) * yb
    x = x + mix @ w_out

    hm = rmsnorm(x, norm_moe).reshape(B * S, D_MODEL)
    x = x + hier_moe(hm, w_rg, b_rg, w_re, b_re, w_eg, w_eu, w_ed).reshape(B, S, D_MODEL)
    return x

def setup_inputs(seed: int = 0) -> dict:
    key = jax.random.key(seed)
    ks = jax.random.split(key, 24)
    nrm = lambda k, shape, s: jax.random.normal(k, shape, jnp.float32) * s
    L = DEPTH
    return {
        'x_prompt': nrm(ks[0], (BATCH, SEQ, D_MODEL), 1.0),
        'x_sample': nrm(ks[1], (DEC_BATCH, DEC_SEQ, D_MODEL), 1.0),
        'norm_mix': 1.0 + nrm(ks[2], (L, D_MODEL), 0.02),
        'w_in': nrm(ks[3], (L, D_MODEL, IN_WIDTH), D_MODEL ** -0.5),
        'rel_bias': nrm(ks[4], (N_REL_BUCKETS, A_HEADS), 0.5),
        'w_gate_f': nrm(ks[5], (L, GATE_RANK, GLA_K_WIDTH), GATE_RANK ** -0.5),
        'b_gate_f': nrm(ks[6], (L, GLA_K_WIDTH), 0.1),
        'w_gate_b': nrm(ks[7], (L, GATE_RANK, GLA_K_WIDTH), GATE_RANK ** -0.5),
        'b_gate_b': nrm(ks[8], (L, GLA_K_WIDTH), 0.1),
        'gla_norm': 1.0 + nrm(ks[9], (L, GLA_DV), 0.02),
        'w_proj_a': nrm(ks[10], (L, A_OUT, D_MODEL), A_OUT ** -0.5),
        'w_proj_b': nrm(ks[11], (L, GLA_V_WIDTH, D_MODEL), GLA_V_WIDTH ** -0.5),
        'w_out': nrm(ks[12], (L, D_MODEL, D_MODEL), D_MODEL ** -0.5),
        'norm_moe': 1.0 + nrm(ks[13], (L, D_MODEL), 0.02),
        'w_router_group': nrm(ks[14], (L, D_MODEL, N_GROUPS), D_MODEL ** -0.5),
        'b_router_group': nrm(ks[15], (L, N_GROUPS), 0.01),
        'w_router_expert': nrm(ks[16], (L, D_MODEL, N_EXPERTS), D_MODEL ** -0.5),
        'b_router_expert': nrm(ks[17], (L, N_EXPERTS), 0.01),
        'w_exp_gate': nrm(ks[18], (L, N_EXPERTS, D_MODEL, EXPERT_FF), D_MODEL ** -0.5),
        'w_exp_up': nrm(ks[19], (L, N_EXPERTS, D_MODEL, EXPERT_FF), D_MODEL ** -0.5),
        'w_exp_down': nrm(ks[20], (L, N_EXPERTS, EXPERT_FF, D_MODEL), EXPERT_FF ** -0.5),
        'norm_final': 1.0 + nrm(ks[21], (D_MODEL,), 0.02),
    }

def reference(x_prompt, x_sample, norm_mix, w_in, rel_bias, w_gate_f, b_gate_f, w_gate_b, b_gate_b,
              gla_norm, w_proj_a, w_proj_b, w_out, norm_moe, w_router_group, b_router_group,
              w_router_expert, b_router_expert, w_exp_gate, w_exp_up, w_exp_down, norm_final):
    def trunk(x):
        for l in range(DEPTH):
            x = encoder_layer(x, norm_mix[l], w_in[l], rel_bias, w_gate_f[l], b_gate_f[l], w_gate_b[l],
                              b_gate_b[l], gla_norm[l], w_proj_a[l], w_proj_b[l], w_out[l], norm_moe[l],
                              w_router_group[l], b_router_group[l], w_router_expert[l], b_router_expert[l],
                              w_exp_gate[l], w_exp_up[l], w_exp_down[l])
        return rmsnorm(x, norm_final)

    y_prompt = trunk(x_prompt)
    y_sample = trunk(x_sample)
    return (y_prompt, y_sample)


_drawn_inputs = setup_inputs


def setup_inputs(seed=0):
    import zlib

    import numpy as np

    out = dict(_drawn_inputs(seed))
    spreads = {}
    factors = {'gla_norm': 3.179,
     'b_router_group': 53.866,
     'b_router_expert': 10.261,
     'norm_final': 7.541}
    for name, (base, spread) in spreads.items():
        noise = np.random.default_rng([zlib.crc32(name.encode()), seed]).standard_normal(out[name].shape)
        drawn = base * np.exp(spread * noise) if base else spread * noise
        out[name] = __import__('jax').numpy.asarray(drawn.astype(out[name].dtype))
    for name, factor in factors.items():
        out[name] = (out[name] * factor).astype(out[name].dtype)
    return out
```

```python
from contextlib import ExitStack

import concourse.bass as bass
from concourse import mybir

F32, F32R, I32, U32 = mybir.dt.float32, mybir.dt.float32r, mybir.dt.int32, mybir.dt.uint32
ALU = mybir.AluOpType
ACT = mybir.ActivationFunctionType
AX = mybir.AxisListType

P = 128
D = 1024
KD = D // P
S_PROMPT, S_SAMPLE = 512, 256
T = S_PROMPT + S_SAMPLE
NT = T // P
HALF = T // 2
SEQS = ((0, S_PROMPT // P), (S_PROMPT // P, S_SAMPLE // P))
NG = 3
AH = 4
HD = 64
AW = AH * HD
GH = 4
DK, DV = 128, 256
CH = 64
NCH = T // CH
RANK = 16
NE, NGRP, EPG, FF = 32, 4, 8, 256
NR = NGRP + NE
WRING = 3
OVER = 11
SLOTS = NE + OVER
NEG = -1e30
EPS = 1e-6
NBK = 32
VEC = 1024
SKIP = 4096
C_QA, C_KA, C_VA = 0, 768, 1536
C_QB, C_KB, C_VB, C_OG = 2304, 2816, 3328, 4352
C_GATE = 5376
C_MA, C_MB = 5408, 6432
BANKS = 8
GW = 256


class Jobs:

    def __init__(self):
        self.by, self.count = [], {"act": 0, "dve": 0}
        self.evac = []

    def new(self, engine):
        self.by.append(engine)
        self.count[engine] += 1
        self.evac.append(self.count[engine])
        return len(self.by) - 1


class Step:

    def __init__(self, kind=None, a=None, b=None, d=None, dest=None, first=None, g=None, h=None, half=None,
                 heads=None, i=None, k=None, ktiles=None, lo=None, n=None, nc=None, q=None, s=None, t=None,
                 u=None, width=None):
        self.kind, self.a, self.b, self.d, self.dest, self.first, self.g = kind, a, b, d, dest, first, g
        self.h, self.half, self.heads, self.i, self.k, self.ktiles, self.lo = h, half, heads, i, k, ktiles, lo
        self.n, self.nc, self.q, self.s, self.t, self.u, self.width = n, nc, q, s, t, u, width
        self.job = self.sc = self.pt = self.pv = self.hi = self.prev = self.seq = None
        self.which = {"kind": kind, "a": a, "d": d, "dest": dest, "first": first, "h": h, "i": i, "s": s}


def interleave(a, b):
    out, j = [], 0
    for i, s in enumerate(a):
        out.append(s)
        while j < len(b) and (j + 1) * len(a) <= (i + 1) * len(b) + len(b) - 1 and j * len(a) < (i + 1) * len(b):
            out.append(b[j])
            j += 1
    return out + b[j:]


def plan():
    steps = []
    S = Step

    def groups():
        g = []
        for a in range(NG):
            g += [("q", a), ("k", a), ("v", a)]
        g += [("gate", 0)]
        for h in range(GH):
            g += [("qkb", h), ("vb", h)]
        g += [("og", h) for h in range(GH)]
        for m in range(4):
            g += [("ma", m), ("pa", m), ("mb", m), ("pb", m)]
        g += [("out", m) for m in range(4)]
        return g

    glist = groups()
    gnum = {g: n for n, g in enumerate(glist)}

    def proj(name, idx):
        n = gnum[name, idx]
        r = []
        if name in ("q", "k"):
            r = [S(kind="ws", g=n, b=b, s=s, dest=(name, idx)) for b in range(2) for s in range(2)]
        elif name == "gate":
            r = [S(kind="ws", g=n, b=0, s=s, dest=(name, idx)) for s in range(2)]
        elif name in ("qkb", "ma", "pa", "mb", "pb"):
            r = [S(kind="ws", g=n, b=b, s=s, dest=(name, idx)) for b in range(2) for s in range(2)]
        elif name in ("v", "vb", "og", "out"):
            r = [S(kind="ts", g=n, i=i, dest=(name, idx)) for i in range(NT)]
        if n + 2 < len(glist):
            r.append(S(kind="w", g=n + 2))
        return r

    steps += [S(kind="vec", a=a, half=h) for a in range(NG) for h in range(2)]
    steps += [S(kind="w", g=0), S(kind="w", g=1)]
    for i in range(NT):
        steps.append(S(kind="norm", i=i))
    for i in range(NT):
        steps += [S(kind="hT", i=i, half=h) for h in range(2)]
    steps += proj("q", 0) + proj("k", 0) + proj("v", 0)

    def units(a):
        u = []
        for first, n in SEQS:
            for t in range(n):
                i = first + t
                if a == 0:
                    lo, hi = (P // 2 if t == 0 else 0), (3 * P // 2 if t == n - 1 else 2 * P)
                    ktiles = [x for x in (i - 1, i, i + 1) if first <= x < first + n]
                    u += [S(a=a, i=i, heads=[h], lo=lo, width=hi - lo, ktiles=ktiles, first=first) for h in range(AH)]
                else:
                    per = 512 // (n * P)
                    u += [S(a=a, i=i, heads=list(range(h, AH, AH // per)), lo=0, width=n * P,
                            ktiles=list(range(first, first + n)), first=first, t=t)
                          for h in range(AH // per)]
        return u

    allu = [units(a) for a in range(NG)]
    flat = [u for x in allu for u in x]
    for n, u in enumerate(flat):
        u.n = n
    for a in range(NG):
        r = []
        us = allu[a]
        for k in range(len(us) + 2):
            if k < len(us):
                r.append(S(kind="sc", u=us[k]))
            if 1 <= k <= len(us):
                r.append(S(kind="pt", u=us[k - 1]))
            if k >= 2:
                r.append(S(kind="pv", u=us[k - 2]))
        if a + 1 < NG:
            other = proj("q", a + 1) + proj("k", a + 1) + proj("v", a + 1)
        else:
            other = proj("gate", 0) + proj("qkb", 0) + proj("vb", 0)
        steps += interleave(r, other)
    steps.append(S(kind="comb"))
    steps += [S(kind="oaT", i=i) for i in range(NT)]

    def chain(h):
        return [S(kind="z", h=h, d=d, s=s) for d in range(2) for s in range(2)] + [S(kind="decay", h=h)]

    def heavy(h):
        r = [S(kind="kot", h=h, q=q) for q in range(3)]
        for first, n in SEQS:
            nc_ = 2 * n
            r += [S(kind="state", h=h, first=first, nc=nc_, t=t, d=d) for t in range(nc_ - 1) for d in range(2)]
            for t in range(n + 1):
                if t < n:
                    r.append(S(kind="intra", h=h, i=first + t, first=first, n=n))
                if t:
                    r.append(S(kind="o", h=h, i=first + t - 1, first=first, n=n))
        return r

    for h in range(GH):
        steps += chain(h)
        if h:
            steps += proj("vb", h)
        if h + 1 < GH:
            steps += proj("qkb", h + 1)
        steps += heavy(h)
    steps.append(S(kind="gstat"))
    for h in range(GH):
        r = proj("og", h)
        steps += r[:NT] + [S(kind="obT", h=h, i=i) for i in range(NT)] + r[NT:]
    for m in range(4):
        for name in ("ma", "pa", "mb", "pb"):
            steps += proj(name, m)
    steps += [S(kind="mixT", k=k) for k in range(KD)]
    for m in range(4):
        steps += proj("out", m)
    for i in range(NT):
        steps += [S(kind="norm2", i=i)]
    for i in range(NT):
        steps += [S(kind="h2T", i=i, half=h) for h in range(2)] + [S(kind="router", i=i)]
    steps += [S(kind="route"), S(kind="rank"), S(kind="place"), S(kind="table")]

    jobs = Jobs()
    act_evacuates = {"q", "k", "v", "gate", "qkb", "vb", "og", "ma", "mb"}
    last_of_group = {}
    for s in steps:
        if s.kind in ("ws", "ts"):
            s.job = jobs.new("act" if s.dest[0] in act_evacuates else "dve")
            last_of_group[s.g] = s.job
        elif s.kind in ("vec", "pv", "z", "kot", "h2T"):
            s.job = jobs.new("act")
        elif s.kind in ("hT", "sc", "oaT", "state", "intra", "o", "obT", "router", "rank", "table"):
            s.job = jobs.new("dve")
        elif s.kind == "pt":
            s.job = jobs.new("act" if s.u.n % 2 else "dve")
        if s.kind == "sc":
            s.u.sc = s.job
        elif s.kind == "pt":
            s.u.pt = s.job
        elif s.kind == "pv":
            s.u.pv = s.job
    n = 0
    for s in steps:
        if s.kind in ("hT", "oaT", "obT"):
            n += 1
            s.hi = n
    prev = {}
    for s in steps:
        if s.kind == "state":
            s.prev = prev.get(s.d)
            prev[s.d] = s.job
    for n, s in enumerate([s for s in steps if s.kind == "o"]):
        s.seq = n
    for n, s in enumerate([s for s in steps if s.kind == "intra"]):
        s.seq = n
    return steps, glist, gnum, flat, jobs, last_of_group


def build(nc, A, outs):
    steps, glist, gnum, units, jobs, last_of_group = plan()
    NU = len(units)
    full = steps
    find = lambda **kw: [s for s in full if all(s.which[k] == v for k, v in kw.items())]
    last_hT = find(kind="hT")[-1].job
    last_pb = last_of_group[gnum["pb", 3]]
    last_out = last_of_group[gnum["out", 3]]
    ctx = ExitStack()
    with ctx:
        BASE = 16512
        KB = 1024

        def at(name, shape, dtype, kb):
            off = BASE + int(kb * KB)
            size = 4
            for x in shape[1:]:
                size *= x
            assert off + size <= 229344, (name, off + size)
            return nc.alloc_sbuf_tensor_at(name, shape, dtype, offset=off)

        small = [0]

        def const(name, shape, dtype=F32):
            t = at(name, shape, dtype, small[0] / KB)
            size = 4
            for x in shape[1:]:
                size *= x
            small[0] += -(-size // 32) * 32
            assert small[0] <= 8 * KB, small[0]
            return t

        ident = const("ident", [P, P])
        mask_f = const("mask_f", [P, P], I32)
        mask_b = const("mask_b", [P, P], I32)
        scan_mask = const("scan_mask", [P, T])
        gate_bias = const("gate_bias", [P, 2, GH])
        ss = const("ss", [P, NT])
        std = const("std", [P, NT])
        rstd = const("rstd", [P, NT])
        mx = const("mx", [P, NT, NG, AH])
        nmx = const("nmx", [P, NT, NG, AH])
        sm = const("sm", [P, NT, NG, AH])
        wgrp = const("wgrp", [P, NT, NG, AH])
        cm = const("cm", [P, NT, AH])
        cden = const("cden", [P, NT, AH])
        gss = const("gss", [P, NT, GH])
        gstd = const("gstd", [P, NT, GH])
        grstd = const("grstd", [P, NT, GH])
        junk_gla = const("junk_gla", [P, DV])
        dec = const("dec", [P, 2, 2, NCH])

        hT_hi = at("hT_hi", [P, KD, T], F32R, 8)
        hT_lo = at("hT_lo", [P, KD, T], F32R, 32)
        raw = at("raw", [P, 2, KD, GW], F32, 56)
        w_hi = at("w_hi", [P, 2, KD, GW], F32R, 72)
        w_lo = at("w_lo", [P, 2, KD, GW], F32R, 88)
        table = [at("table0", [P, AH, 2 * P], F32, 132), at("table1", [P, AH, 896], F32, 104),
                 at("table2", [P, AH, 896], F32, 118)]
        onehot = at("onehot", [NBK + 1, NG, VEC], F32, 118)
        vecs = at("vecs", [AH, NG, VEC], F32, 148)
        relx = at("relx", [NBK + 1, NG * AH], F32, 131.5)
        xin = at("xin", [P, NT, D], F32, 172)
        g_mix = at("g_mix", [P, D], F32, 196)
        junk = at("junk", [P, D], F32, 200)
        qk = at("qk", [P, 2, 4, T], F32, 136)
        va = at("va", [P, 2, NT, AW], F32, 160)
        o_att = at("o_att", [P, NT, NG, AW], F32, 172)
        pad = at("pad", [P, 2, 3 * P], F32, 190)
        sc = at("sc", [P, 3, 512], F32, 193)
        ptr = at("ptr", [P, 3, 512], F32, 199)
        oaT_hi = at("oaT_hi", [P, 2, T], F32R, 104)
        oaT_lo = at("oaT_lo", [P, 2, T], F32R, 110)
        o_gla = at("o_gla", [P, NT, D], F32, 116)
        qkb = [at("qkb0", [P, 2, T], F32, 148), at("qkb1", [P, 2, T], F32, 140)]
        vb = at("vb", [P, NT, DV], F32, 154)
        ptg = at("ptg", [P, 2, P], F32, 146)
        wgate = at("wgate", [2 * RANK, 2, P], F32, 147)
        zt = at("zt", [P, 2, T], F32, 160)
        gT = at("gT", [2 * RANK, T], F32, 166)
        et = at("et", [P, 2, T], F32, 169)
        q_in = at("q_in", [P, 2, T], F32, 175)
        k_in = at("k_in", [P, 2, T], F32, 181)
        kot = at("kot", [P, 12, P], F32, 187)
        st = at("st", [P, 2, 7, DV], F32, 193)
        obT_hi = at("obT_hi", [P, KD, T], F32R, 140)
        obT_lo = at("obT_lo", [P, KD, T], F32R, 164)
        sg = at("sg", [P, 2, DV], F32, 188)
        g_gla = at("g_gla", [P, DV], F32, 190)
        sga = at("sga", [P, 2, T], F32, 191)
        sgb = at("sgb", [P, 2, T], F32, 197)
        mixf = at("mixf", [P, KD, T], F32, 116)
        mT_hi = at("mT_hi", [P, KD, T], F32R, 8)
        mT_lo = at("mT_lo", [P, KD, T], F32R, 32)
        x1 = at("x1", [P, NT, D], F32, 140)
        junk2 = at("junk2", [P, D], F32, 164)
        h2 = at("h2", [P, NT, D], F32, 168)
        g_moe = at("g_moe", [P, D], F32, 192)
        h2T = at("h2T", [P, 2, KD, P], F32, 196)
        wr = at("wr", [P, KD, NR], F32, 204)
        r_bias = at("r_bias", [P, NR], F32, 205.5)

        route_kb = [136.0]

        def route(name, shape, dtype=F32):
            t = at(name, shape, dtype, route_kb[0])
            size = 4
            for x in shape[1:]:
                size *= x
            route_kb[0] += -(-size // 32) * 32 / KB
            return t

        earlier = route("earlier", [P, P])
        ones = route("ones", [P, P])
        iota_row = route("iota_row", [P, P])
        iota_tok = route("iota_tok", [P, NT])
        l_grp = route("l_grp", [P, NT, 8])
        l_exp = route("l_exp", [P, NT, NE])
        slot_idx = route("slot_idx", [P, SLOTS], I32)
        pair_idx = route("pair_idx", [P, NT, 2], I32)
        pair_w = route("pair_w", [P, NT, 2])
        over_row = route("over_row", [1, OVER + 1], I32)
        x_idx = route("x_idx", [P, 2], I32)
        assert route_kb[0] <= 140
        route_kb[0] = 196.0
        top = route("top", [P, NT, 8])
        top_at = route("top_at", [P, NT, 8], U32)
        top2 = route("top2", [P, NT, 8])
        top2_at = route("top2_at", [P, NT, 8], U32)
        g_at = route("g_at", [P, NT])
        e_at = route("e_at", [P, NT, 2])
        p_grp = route("p_grp", [P, NT])
        ratio = route("ratio", [P, NT])
        ex = route("ex", [P, NT, 8])
        l_sel = route("l_sel", [P, NT, EPG])
        hot = [route("hot0", [P, NT, NE]), route("hot1", [P, NT, NE])]
        both = route("both", [P, NT, NE])
        rank = route("rank", [P, NT, NE])
        tally = route("tally", [P, NE])
        n_over_e = route("n_over_e", [P, NE])
        over_end = route("over_end", [P, NE])
        shift = route("shift", [P, NE])
        pos = route("pos", [P, NT, 2])
        pos_i = route("pos_i", [P, NT, 2], I32)
        row_i = route("row_i", [P, NT, 2], I32)
        row_f = route("row_f", [P, NT, 2])
        slot_f = route("slot_f", [P, NT, 2])
        tab = route("tab", [P, SLOTS])
        tab0 = route("tab0", [P, SLOTS])
        over_cmp = route("over_cmp", [1, OVER, NE])
        over_f = route("over_f", [1, OVER + 1])
        assert route_kb[0] <= 203.75, route_kb
        row_hot = at("row_hot", [P, 2 * NT, P], F32, 172)
        slot_hot = at("slot_hot", [P, 2 * NT, SLOTS], F32, 178)
        kinds = ("gate", "up", "down")
        m_raw, m_hi, m_lo = {}, {}, {}
        for n, x in enumerate(kinds):
            shape = [2, D] if x == "down" else [KD, FF]
            m_raw[x] = at(f"raw_{x}", [P, WRING] + shape, F32, 8 + 24 * n)
            m_lo[x] = at(f"lo_{x}", [P, WRING] + shape, F32R, 8 + 24 * n)
            m_hi[x] = at(f"hi_{x}", [P, 2] + shape, F32R, 80 + 16 * n)
        m_x = at("m_x", [P, 2, D], F32, 128)
        m_y = at("m_y", [P, 2, D], F32, 164)
        m_xT_hi = at("m_xT_hi", [P, 2, KD, P], F32R, 172)
        m_xT_lo = at("m_xT_lo", [P, 2, KD, P], F32R, 180)
        m_a = at("m_a", [P, 2, FF], F32, 188)
        m_sil = at("m_sil", [P, 2, FF], F32, 190)
        m_aT_hi = at("m_aT_hi", [P, 2, 2, P], F32R, 192)
        m_aT_lo = at("m_aT_lo", [P, 2, 2, P], F32R, 194)
        g_fin = at("g_fin", [P, D], F32, 203.75)
        y_pair = at("y_pair", [P, 2, 2, D], F32, 32)
        y_fin = at("y_fin", [P, 2, D], F32, 48)
        junk3 = at("junk3", [P, D], F32, 56)

        psum = [ctx.enter_context(nc.psum_tensor(f"bank{b}", [P, 512], F32)) for b in range(BANKS)]
        bank = lambda job: psum[job % BANKS]

        vec_d = nc.dram_tensor("vec_d", (NG * AH, VEC), F32, kind="Internal").ap()
        rep_d = nc.dram_tensor("rep_d", (NG * AH * P, VEC), F32, kind="Internal").ap()
        h2_d = nc.dram_tensor("h2_d", (T, D), F32, kind="Internal").ap()
        y_d = nc.dram_tensor("y_d", (SLOTS * P, D), F32, kind="Internal").ap()

        def sem(name):
            return ctx.enter_context(nc.semaphore(name))

        x_in = [sem(f"x_in{i}") for i in range(NT)]
        rel_in, gmix_in, small_in, gate_in, ggla_in, moe_in = (
            sem("rel_in"), sem("gmix_in"), sem("small_in"), sem("gate_in"), sem("ggla_in"), sem("moe_in"))
        raw_in = [sem("raw_in0"), sem("raw_in1")]
        wg_in = sem("wg_in")
        vec_out, rep_out, table_in = sem("vec_out"), sem("rep_out"), sem("table_in")
        consts = sem("consts")
        mm = sem("mm")
        act_evac, dve_evac = sem("act_evac"), sem("dve_evac")
        whi_done, wlo_done = sem("whi_done"), sem("wlo_done")
        hi_done = sem("hi_done")
        sq_done, var_done, std_done, xn_done = sem("sq_done"), sem("var_done"), sem("std_done"), sem("xn_done")
        pad_zero, neg_max, probs = sem("pad_zero"), sem("neg_max"), sem("probs")
        comb_neg, comb_exp, oa_done = sem("comb_neg"), sem("comb_exp"), sem("oa_done")
        softplus, cum, e1, qin, e2, kin, e3, ko = (sem(x) for x in ("softplus", "cum", "e1", "qin", "e2", "kin", "e3", "ko"))
        dd = sem("dd")
        gla_sq, gvar, gstd_done, ob_done = sem("gla_sq"), sem("gvar"), sem("gstd_done"), sem("ob_done")
        mhi_done, mlo_done = sem("mhi_done"), sem("mlo_done")
        x1_in = [sem(f"x1_in{i}") for i in range(NT)]
        sq2, var2, std2, h2_done, h2_out = sem("sq2"), sem("var2"), sem("std2"), sem("h2_done"), sem("h2_out")
        act_chain, dve_chain, pool_chain, pe_chain = sem("act_chain"), sem("dve_chain"), sem("pool_chain"), sem("pe_chain")
        rconst, route_neg, route_exp, route_neg2, route_exp2 = (
            sem("rconst"), sem("route_neg"), sem("route_exp"), sem("route_neg2"), sem("route_exp2"))
        hot_done, place_done, over_done = sem("hot_done"), sem("place_done"), sem("over_done")
        w_arrived = {x: [sem(f"arrived_{x}{r}") for r in range(WRING)] for x in kinds}
        w_hi_done = {x: sem(f"hi_{x}_done") for x in kinds}
        w_lo_done = {x: sem(f"lo_{x}_done") for x in kinds}
        x_copied, x_gathered = sem("x_copied"), [sem("x_gathered0"), sem("x_gathered1")]
        xt_mm, xt_hi, xt_lo = sem("xt_mm"), sem("xt_hi"), sem("xt_lo")
        gu_mm, silu_done, a_done = sem("gu_mm"), sem("silu_done"), sem("a_done")
        at_mm, at_hi, at_lo = sem("at_mm"), sem("at_hi"), sem("at_lo")
        y_mm, y_done = sem("y_mm"), sem("y_done")
        y_out = [sem("y_out0"), sem("y_out1")]
        results_in, zero_out = sem("results_in"), sem("zero_out")
        gfin_in = sem("gfin_in")
        pair_in = [sem("pair_in0"), sem("pair_in1")]
        sum_done, sq3, var3, std3, fin_done = sem("sum_done"), sem("sq3"), sem("var3"), sem("std3"), sem("fin_done")
        out_done = [sem("out_done0"), sem("out_done1")]

        B_XT, B_GU, B_AT, B_Y = (0, 1), (2, 3), (4, 7), (5, 6)

        LOOPED = 4
        FIRST, TURN = 2, 2 * WRING

        def first_tiles(eng_fori, body):
            def one(e):
                body(e, e % 2, e // 2, e % WRING, e // WRING)

            for e in range(FIRST):
                one(e)
            with eng_fori(0, LOOPED) as turn:
                for c in range(FIRST, FIRST + TURN):
                    body(turn * TURN + c, c % 2, turn * WRING + c // 2, c % WRING, turn * 2 + c // WRING)
            for e in range(FIRST + LOOPED * TURN, NE):
                one(e)

        def later(r, u, n):
            return (r + n) % WRING, u + (r + n) // WRING

        def ahead(e, n):
            return not isinstance(e, int) or e + n < NE

        def first(e):
            return isinstance(e, int) and e == 0

        def beyond(eng, body):
            eng.wait_ge(over_done, 1)
            n_over = eng.value_load(over_row[0:1, OVER:OVER + 1], min_val=0, max_val=OVER)
            with eng.Fori(0, OVER) as j:
                with eng.If(n_over > j):
                    body(j + NE, j, j + NE // 2, j + (NE - 1) // WRING + 1)
            return n_over

        seen = {}

        def need(who, eng, s, value):
            if seen.get((eng, s.name), 0) < value:
                seen[eng, s.name] = value
                who.wait_ge(s, value)

        counts = {"act": 0, "dve": 0, "pool": 0}
        chains = {"act": act_chain, "dve": dve_chain, "pool": pool_chain}

        def evac_done(who, eng, job):
            by = jobs.by[job]
            need(who, eng, act_evac if by == "act" else dve_evac, jobs.evac[job])

        def evac_sem(job):
            return act_evac if jobs.by[job] == "act" else dve_evac

        def x_rows(i):
            if i < S_PROMPT // P:
                return A["x_prompt"][0, i * P:(i + 1) * P, :]
            i -= S_PROMPT // P
            return A["x_sample"][0, i * P:(i + 1) * P, :]

        def bcast(ap1d, n):
            return bass.AP(ap1d.tensor, ap1d.offset, [[0, P], [1, n]])

        def group_parts(g):
            name, a = glist[g]
            w_in = A["w_in"][0]
            cols = {"q": C_QA, "k": C_KA, "v": C_VA, "vb": C_VB, "og": C_OG, "ma": C_MA, "mb": C_MB}
            if name in cols:
                return [(w_in[:, cols[name] + GW * a:cols[name] + GW * (a + 1)], KD, 0, GW)]
            if name == "gate":
                return [(w_in[:, C_GATE:C_GATE + 2 * RANK], KD, 0, 2 * RANK)]
            if name == "qkb":
                return [(w_in[:, C_QB + DK * a:C_QB + DK * (a + 1)], KD, 0, DK),
                        (w_in[:, C_KB + DK * a:C_KB + DK * (a + 1)], KD, DK, DK)]
            src = {"pa": A["w_proj_a"], "pb": A["w_proj_b"], "out": A["w_out"]}[name][0]
            return [(src[:, GW * a:GW * (a + 1)], 2 if name == "pa" else KD, 0, GW)]

        raw_value = {}
        total = [0, 0]
        for g in range(len(glist)):
            total[g % 2] += 16 * len(group_parts(g))
            raw_value[g] = total[g % 2]

        def group_shape(g):
            name, _ = glist[g]
            return (2 if name == "pa" else KD), (2 * RANK if name == "gate" else GW)

        block = ctx.enter_context(nc.Block())

        @block.sync
        def _(sp):
            E_ = "sp"
            sp.dma_start(onehot[:, :, :], A["const_buckets"].rearrange("b (a n) -> b a n", a=NG)).then_inc(rel_in, 16)
            sp.dma_start(relx[0:NBK, :], A["rel_bias"]).then_inc(rel_in, 16)
            sp.dma_start(xin[:, 0, :], x_rows(0)).then_inc(x_in[0], 16)
            sp.dma_start(g_mix[:, :], bcast(A["norm_mix"], D)).then_inc(gmix_in, 16)
            for i in range(1, NT):
                sp.dma_start(xin[:, i, :], x_rows(i)).then_inc(x_in[i], 16)
            for d, name in enumerate(("b_gate_f", "b_gate_b")):
                sp.dma_start(gate_bias[:, d, :], A[name][0].rearrange("(h p) -> p h", p=P),
                             allow_slow_non_contiguous=True).then_inc(small_in, 16)
            for s in steps:
                if s.kind == "w":
                    g = s.g
                    if g >= 2:
                        need(sp, E_, wlo_done, g - 1)
                    for src, kb, c0, n in group_parts(g):
                        sp.dma_start(raw[:, g % 2, 0:kb, c0:c0 + n],
                                     src.rearrange("(k p) n -> p k n", p=P)).then_inc(raw_in[g % 2], 16)
                if s.kind == "ts" and s.dest == ("out", 0) and s.i == 0:
                    evac_done(sp, E_, last_pb)
                    for i in range(NT):
                        sp.dma_start(x1[:, i, :], x_rows(i)).then_inc(x1_in[i], 16)
                    sp.dma_start(g_moe[:, :], bcast(A["norm_moe"], D)).then_inc(moe_in, 16)
                    sp.dma_start(wr[:, :, 0:NGRP], A["w_router_group"][0].rearrange("(k p) n -> p k n", p=P)).then_inc(moe_in, 16)
                    sp.dma_start(wr[:, :, NGRP:NR], A["w_router_expert"][0].rearrange("(k p) n -> p k n", p=P)).then_inc(moe_in, 16)
                    sp.dma_start(r_bias[:, 0:NGRP], bcast(A["b_router_group"], NGRP)).then_inc(moe_in, 16)
                    sp.dma_start(r_bias[:, NGRP:NR], bcast(A["b_router_expert"], NE)).then_inc(moe_in, 16)
            src = {"gate": A["w_exp_gate"][0].rearrange("e (k p) n -> p e k n", p=P),
                   "up": A["w_exp_up"][0].rearrange("e (k p) n -> p e k n", p=P),
                   "down": A["w_exp_down"][0].rearrange("e (k p) n -> p e k n", p=P)}
            y_rows = y_d.rearrange("(s p) n -> p s n", p=P)

            def load(expert, e, r):
                for x in kinds:
                    if not (isinstance(e, int) and e < WRING):
                        sp.wait_ge(y_mm if x == "down" else gu_mm, e - WRING + 1 if r is not None else e)
                    slot = r or 0
                    sp.dma_start(m_raw[x][:, slot], src[x][:, bass.ds(expert, 1), :, :].rearrange("p e k n -> p (e k) n"))\
                      .then_inc(w_arrived[x][slot], 16)

            def store(e, p):
                sp.wait_ge(y_done, e + 1)
                sp.dma_start(y_rows[:, bass.ds(e, 1), :].rearrange("p s n -> p (s n)"), m_y[:, p, :]).then_inc(y_out[p], 16)

            need(sp, E_, mm, last_out + 1)
            sp.wait_ge(rconst, 1)
            sp.dma_start(y_rows[:, NE:SLOTS, :],
                         m_x[:, 0:1, :].broadcast_to([P, OVER, D])).then_inc(zero_out, 16)
            for e in range(WRING):
                load(e, e, e)

            def tile(e, p, k, r, u):
                if ahead(e, WRING):
                    load(e + WRING, e + WRING, r)
                store(e, p)

            first_tiles(sp.Fori, tile)
            sp.wait_ge(mm, len(jobs.by))
            sp.wait_ge(over_done, 1)
            sp.dma_start(g_fin[:, :], bcast(A["norm_final"], D)).then_inc(gfin_in, 16)

            def beyond_tile(e, j, k, u):
                expert = sp.value_load(over_row[0:1, bass.ds(j, 1)], min_val=0, max_val=NE - 1)
                load(expert, e, None)
                store(e, 0)

            beyond(sp, beyond_tile)
            for i in range(NT):
                sp.wait_ge(fin_done, i + 1)
                out, r = (outs[0], i) if i < S_PROMPT // P else (outs[1], i - S_PROMPT // P)
                sp.dma_start(out[0, r * P:(r + 1) * P, :], y_fin[:, i % 2, :]).then_inc(out_done[i % 2], 16)
            for p in range(2):
                sp.wait_ge(out_done[p], 16 * NT // 2)

        @block.gpsimd
        def _(pool):
            E_ = "pool"

            def link(ins):
                counts["pool"] += 1
                ins.then_inc(pool_chain, 1)
                pool.wait_ge(pool_chain, counts["pool"])

            pool.memset(relx[NBK:NBK + 1, :], 1.0).then_inc(consts, 1)
            pool.wait_ge(consts, 1)
            link(pool.memset(ident[:, :], 0.0))
            link(pool.affine_select(out=ident[:, :], in_=ident[:, :], compare_op=ALU.not_equal, fill=1.0,
                                    base=0, pattern=[[-1, P]], channel_multiplier=1))
            link(pool.memset(mask_f[:, :], 1))
            link(pool.memset(mask_b[:, :], 1))
            link(pool.affine_select(out=mask_f[:, :], in_=mask_f[:, :], compare_op=ALU.is_ge, fill=0,
                                    base=0, pattern=[[1, P]], channel_multiplier=-1))
            link(pool.affine_select(out=mask_b[:, :], in_=mask_b[:, :], compare_op=ALU.is_ge, fill=0,
                                    base=-1, pattern=[[-1, P]], channel_multiplier=1))
            link(pool.memset(mask_f[0:CH, CH:P], 0))
            link(pool.memset(mask_b[CH:P, 0:CH], 0))
            link(pool.memset(scan_mask[:, :], 1.0))
            link(pool.memset(scan_mask[:, :].rearrange("p (c t) -> p c t", t=CH)[:, :, 0:1], 0.0))
            pool.memset(scan_mask[:, 0:1], 0.0).then_inc(consts, 1)
            pool.wait_ge(consts, 2)
            need(pool, E_, act_evac, jobs.evac[find(kind="vec")[-1].job])
            pool.dma_start(vec_d.rearrange("(a h) n -> h a n", a=NG), vecs[:, :, :]).then_inc(vec_out, 16)
            pool.wait_ge(vec_out, 16)
            pool.dma_start(bass.AP(rep_d.tensor, 0, [[P * VEC, NG * AH], [VEC, P], [1, VEC]]),
                           bass.AP(vec_d.tensor, 0, [[VEC, NG * AH], [0, P], [1, VEC]])).then_inc(rep_out, 16)
            pool.wait_ge(rep_out, 16)
            for a in range(NG):
                start, width = (447, 2 * P) if a == 0 else (127, 896)
                pool.dma_start(table[a][:, :, :],
                               bass.AP(rep_d.tensor, a * AH * P * VEC + start,
                                       [[VEC - 1, P], [P * VEC, AH], [1, width]])).then_inc(table_in, 16)

            pads, gs, mls = [0], [0], [0]
            for s in steps:
                if s.kind == "w":
                    gs[0] = s.g + 1
                    g = s.g
                    kb, n = group_shape(g)
                    need(pool, E_, whi_done, g + 1)
                    need(pool, E_, wlo_done, g)
                    need(pool, E_, mlo_done, mls[0])
                    need(pool, E_, pad_zero, pads[0])
                    pool.tensor_tensor(w_lo[:, g % 2, 0:kb, 0:n], raw[:, g % 2, 0:kb, 0:n],
                                       w_hi[:, g % 2, 0:kb, 0:n].bitcast(F32), ALU.subtract).then_inc(wlo_done, 1)
                elif s.kind == "sc" and s.u.n == 0:
                    need(pool, E_, mm, last_hT + 1)
                    need(pool, E_, dve_evac, jobs.evac[last_hT])
                    need(pool, E_, wlo_done, gs[0])
                    pads[0] = 1
                    link(pool.memset(pad[:, :, 0:CH], 0.0))
                    pool.memset(pad[:, :, 3 * P - CH:3 * P], 0.0).then_inc(pad_zero, 1)
                elif s.kind == "z" and s.d == 0 and s.s == 0:
                    h = s.h
                    if h == 0:
                        need(pool, E_, mm, units[-1].sc + 1)
                        need(pool, E_, wlo_done, gs[0])
                        link(pool.memset(wgate[:, :, :], 0.0))
                        link(pool.memset(ptg[:, :, :], 0.0))
                    else:
                        need(pool, E_, mm, find(kind="z", h=h - 1)[-1].job + 1)
                    pool.dma_start(wgate[0:RANK, 0, :], A["w_gate_f"][0][:, h * DK:(h + 1) * DK]).then_inc(wg_in, 16)
                    pool.dma_start(wgate[RANK:2 * RANK, 1, :], A["w_gate_b"][0][:, h * DK:(h + 1) * DK]).then_inc(wg_in, 16)
                elif s.kind == "gstat":
                    need(pool, E_, mm, find(kind="o")[-1].job + 1)
                    pool.dma_start(g_gla[:, :], bcast(A["gla_norm"], DV)).then_inc(ggla_in, 16)
                elif s.kind == "mixT":
                    need(pool, E_, wlo_done, gs[0])
                    need(pool, E_, mlo_done, s.k)
                    mls[0] = s.k + 1
                    need(pool, E_, mhi_done, s.k + 1)
                    pool.tensor_tensor(mT_lo[:, s.k, :], mixf[:, s.k, :], mT_hi[:, s.k, :].bitcast(F32),
                                       ALU.subtract).then_inc(mlo_done, 1)
                elif s.kind == "norm2" and s.i == 0:
                    need(pool, E_, mm, last_out + 1)
                    need(pool, E_, mlo_done, KD)
                    link(pool.memset(m_x[:, :, :], 0.0))
                    link(pool.memset(ones[:, :], 1.0))
                    link(pool.memset(earlier[:, :], 1.0))
                    link(pool.affine_select(out=earlier[:, :], in_=earlier[:, :], compare_op=ALU.is_ge, fill=0.0,
                                            base=-1, pattern=[[1, P]], channel_multiplier=-1))
                    link(pool.iota(iota_row[:, :], pattern=[[1, P]], base=0, channel_multiplier=0,
                                   allow_small_or_imprecise_dtypes=True))
                    pool.iota(iota_tok[:, :], pattern=[[P, NT]], base=1, channel_multiplier=1,
                              allow_small_or_imprecise_dtypes=True).then_inc(rconst, 1)
                    pool.wait_ge(rconst, 1)
                elif s.kind == "h2T" and s.half == 0:
                    need(pool, E_, h2_done, s.i + 1)
                    pool.dma_start(h2_d[s.i * P:(s.i + 1) * P, :], h2[:, s.i, :]).then_inc(h2_out, 16)

            for e in range(2):
                for x in kinds:
                    need(pool, E_, w_hi_done[x], e + 1)
                    pool.tensor_tensor(m_lo[x][:, e], m_raw[x][:, e], m_hi[x][:, e].bitcast(F32),
                                       ALU.subtract).then_inc(w_lo_done[x], 1)
                    need(pool, E_, w_lo_done[x], e + 1)
            evac_done(pool, E_, find(kind="table")[0].job)

            def take_idx(e, p, ring):
                if not (isinstance(e, int) and e < ring):
                    pool.wait_ge(xt_mm, e + (1 - ring))
                pool.tensor_copy(x_idx[:, p:p + 1], slot_idx[:, bass.ds(e, 1)]).then_inc(x_copied, 1)

            def lo_gate(e, p, r, copied):
                pool.wait_ge(w_hi_done["gate"], e + 1)
                pool.wait_ge(x_copied, copied)
                pool.tensor_tensor(m_lo["gate"][:, r], m_raw["gate"][:, r], m_hi["gate"][:, p].bitcast(F32),
                                   ALU.subtract).then_inc(w_lo_done["gate"], 1)

            def gather(p):
                pool.indirect_dma_start(m_x[:, p, :], None, h2_d,
                                        bass.IndirectOffsetOnAxis(ap=x_idx[:, p:p + 1].bitcast(U32), axis=0),
                                        bounds_check=T - 1, oob_is_err=False).then_inc(x_gathered[p], 16)

            pool.wait_ge(h2_out, 16 * NT)
            pool.wait_ge(zero_out, 16)
            take_idx(0, 0, 2)
            pool.wait_ge(x_copied, 1)
            gather(0)
            take_idx(1, 1, 2)
            pool.wait_ge(x_copied, 2)
            gather(1)
            take_idx(2, 0, 2)
            pool.wait_ge(x_copied, 3)
            gather(0)

            def tile(e, p, k, r, u):
                if ahead(e, 3):
                    pool.wait_ge(w_lo_done["gate"], e + 2)
                    take_idx(e + 3, 1 - p, 2)
                if ahead(e, 2):
                    lo_gate(e + 2, p, later(r, u, 2)[0], e + 4 if ahead(e, 3) else NE)
                if ahead(e, 3):
                    gather(1 - p)

            first_tiles(pool.Fori, tile)

            def beyond_tile(e, j, k, u):
                pool.wait_ge(w_lo_done["gate"], e)
                take_idx(e, 0, 1)
                lo_gate(e, 0, 0, e + 1)
                gather(0)

            n_over = beyond(pool, beyond_tile)
            pool.wait_ge(y_out[0], (n_over + NE // 2) * 16)
            pool.wait_ge(y_out[1], NE // 2 * 16)
            pool.sem_inc(results_in, 1)
            pool.wait_ge(results_in, 1)
            pool.wait_ge(place_done, 1)
            for i in range(NT):
                if i >= 2:
                    pool.wait_ge(sum_done, i - 1)
                for j in range(2):
                    pool.indirect_dma_start(y_pair[:, i % 2, j, :], None, y_d,
                                            bass.IndirectOffsetOnAxis(ap=pair_idx[:, i, j:j + 1].bitcast(U32), axis=0),
                                            bounds_check=SLOTS * P - 1, oob_is_err=False).then_inc(pair_in[i % 2], 16)

        @block.scalar
        def _(act):
            E_ = "act"

            def mark(ins):
                counts["act"] += 1
                ins.then_inc(act_chain, 1)

            def settle():
                need(act, E_, act_chain, counts["act"])

            def hi_weights(x, e, p, ring, r, u):
                act.wait_ge(w_arrived[x][r], u * 16 + 16)
                if not (isinstance(e, int) and e < ring):
                    act.wait_ge(y_mm if x == "down" else gu_mm, e + (1 - ring))
                act.activation(m_hi[x][:, p], m_raw[x][:, r], ACT.Copy).then_inc(w_hi_done[x], 1)

            for s in steps:
                k = s.kind
                if k == "w":
                    g = s.g
                    kb, n = group_shape(g)
                    need(act, E_, raw_in[g % 2], raw_value[g])
                    if g >= 2:
                        need(act, E_, mm, last_of_group[g - 2] + 1)
                    act.activation(w_hi[:, g % 2, 0:kb, 0:n], raw[:, g % 2, 0:kb, 0:n], ACT.Copy).then_inc(whi_done, 1)
                elif k == "vec":
                    need(act, E_, mm, s.job + 1)
                    act.activation(vecs[:, s.a, s.half * 512:(s.half + 1) * 512], bank(s.job)[0:AH, :], ACT.Copy)\
                       .then_inc(act_evac, 1)
                elif k == "norm":
                    i = s.i
                    need(act, E_, sq_done, i)
                    need(act, E_, x_in[i], 16)
                    act.activation(junk[:, :], xin[:, i, :], ACT.Square, accum_out=ss[:, i:i + 1]).then_inc(sq_done, 1)
                    need(act, E_, var_done, i + 1)
                    act.activation(std[:, i:i + 1], rstd[:, i:i + 1], ACT.Sqrt).then_inc(std_done, 1)
                elif k in ("hT", "oaT", "obT"):
                    need(act, E_, mm, s.job + 1)
                    if k == "hT":
                        out, src = hT_hi[:, 4 * s.half:4 * s.half + 4, s.i * P:(s.i + 1) * P], bank(s.job)[:, :]
                    elif k == "oaT":
                        out, src = oaT_hi[:, :, s.i * P:(s.i + 1) * P], bank(s.job)[:, 0:2 * P]
                    else:
                        out, src = obT_hi[:, 2 * s.h:2 * s.h + 2, s.i * P:(s.i + 1) * P], bank(s.job)[:, 0:2 * P]
                    act.activation(out, src.rearrange("p (k t) -> p k t", t=P), ACT.Copy).then_inc(hi_done, 1)
                elif k in ("ws", "ts") and jobs.by[s.job] == "act":
                    name, a = s.dest
                    need(act, E_, mm, s.job + 1)
                    b_ = bank(s.job)
                    if k == "ws":
                        src, tok = b_[:, 0:HALF], slice(s.s * HALF, (s.s + 1) * HALF)
                        if name == "q":
                            act.activation(qk[:, a % 2, s.b, tok], src, ACT.Copy, scale=HD ** -0.5).then_inc(act_evac, 1)
                        elif name == "k":
                            act.activation(qk[:, a % 2, 2 + s.b, tok], src, ACT.Copy).then_inc(act_evac, 1)
                        elif name == "gate":
                            act.activation(gT[:, tok], b_[0:2 * RANK, 0:HALF], ACT.Copy).then_inc(act_evac, 1)
                        elif name == "qkb":
                            if a >= 2:
                                need(act, E_, ko, 2 * (a - 2) + 2)
                            act.activation(qkb[a % 2][:, s.b, tok], src, ACT.Copy).then_inc(act_evac, 1)
                        else:
                            if a:
                                need(act, E_, dve_evac, jobs.evac[last_of_group[gnum["pb", a - 1]]])
                            act.activation((sga if name == "ma" else sgb)[:, s.b, tok], src, ACT.Sigmoid)\
                               .then_inc(act_evac, 1)
                    else:
                        src = b_[:, 0:GW]
                        if name == "v":
                            act.activation(va[:, a % 2, s.i, :], src, ACT.Copy).then_inc(act_evac, 1)
                        elif name == "vb":
                            act.activation(vb[:, s.i, :], src, ACT.Copy).then_inc(act_evac, 1)
                        else:
                            n = NT * a + s.i
                            if n >= 2:
                                need(act, E_, ob_done, n - 1)
                            act.activation(sg[:, n % 2, :], src, ACT.Silu).then_inc(act_evac, 1)
                elif k == "sc":
                    u = s.u
                    need(act, E_, neg_max, u.n + 1)
                    for hh, h in enumerate(u.heads):
                        if u.a == 0:
                            if u.n >= 2:
                                need(act, E_, mm, units[u.n - 2].pt + 1)
                            out = pad[:, u.n % 2, CH + u.lo:CH + u.lo + u.width]
                        else:
                            out = sc[:, u.n % 3, hh * u.width:(hh + 1) * u.width]
                        ins = act.activation(out, sc[:, u.n % 3, hh * u.width:(hh + 1) * u.width], ACT.Exp,
                                             bias=nmx[:, u.i, u.a, h:h + 1], accum_out=sm[:, u.i, u.a, h:h + 1])
                    ins.then_inc(probs, 1)
                elif k == "pt" and jobs.by[s.job] == "act":
                    u = s.u
                    n = len(u.heads) * len(u.ktiles) * P
                    need(act, E_, mm, s.job + 1)
                    act.activation(ptr[:, u.n % 3, 0:n], bank(s.job)[:, 0:n], ACT.Copy).then_inc(act_evac, 1)
                elif k == "pv":
                    u = s.u
                    nh, hs = len(u.heads), slice(u.heads[0], u.heads[-1] + 1, 2)
                    need(act, E_, mm, s.job + 1)
                    act.activation(o_att[:, u.i, u.a, :].rearrange("p (h d) -> p h d", d=HD)[:, hs, :],
                                   bank(s.job)[:, 0:nh * HD].rearrange("p (h d) -> p h d", d=HD), ACT.Copy)\
                       .then_inc(act_evac, 1)
                elif k == "comb":
                    need(act, E_, comb_neg, 1)
                    act.activation(nmx[:, :, :, :], mx[:, :, :, :], ACT.Exp).then_inc(comb_exp, 1)
                elif k == "z":
                    need(act, E_, mm, s.job + 1)
                    if s.h:
                        need(act, E_, ko, 2 * s.h)
                    act.activation(zt[:, s.d, s.s * HALF:(s.s + 1) * HALF], bank(s.job)[:, 0:HALF], ACT.Identity,
                                   bias=gate_bias[:, s.d, s.h:s.h + 1]).then_inc(act_evac, 1)
                elif k == "decay":
                    h = s.h
                    if h:
                        need(act, E_, mm, find(kind="kot", h=h - 1)[-1].job + 1)
                    for d in range(2):
                        need(act, E_, act_evac, jobs.evac[find(kind="z", h=h, d=d, s=1)[0].job])
                        mark(act.activation(et[:, d, :], zt[:, d, :], ACT.Abs))
                    settle()
                    for d in range(2):
                        mark(act.activation(et[:, d, :], et[:, d, :], ACT.Exp, scale=-1.0))
                    settle()
                    for d in range(2):
                        act.activation(et[:, d, :], et[:, d, :], ACT.Ln, bias=1.0).then_inc(softplus, 1)
                    for d in range(2):
                        need(act, E_, cum, 2 * h + d + 1)
                        last = zt[:, d, :].rearrange("p (c t) -> p c t", t=CH)[:, :, (CH - 1 if d == 0 else 0)]
                        act.activation(et[:, d, :], zt[:, d, :], ACT.Exp, scale=1.0 / 16).then_inc(e1, 1)
                        act.activation(dec[:, h % 2, d, :], last, ACT.Exp, scale=1.0 / 16).then_inc(e1, 1)
                    for d in range(2):
                        need(act, E_, qin, 2 * h + d + 1)
                        act.activation(et[:, d, :], zt[:, d, :], ACT.Exp, scale=-1.0 / 16).then_inc(e2, 1)
                    for d in range(2):
                        need(act, E_, dd, 2 * h + d + 1)
                        act.activation(et[:, d, :], et[:, d, :], ACT.Exp, scale=1.0 / 16).then_inc(e3, 1)
                elif k == "kot":
                    need(act, E_, mm, s.job + 1)
                    act.activation(kot[:, 4 * s.q:4 * s.q + 4, :].rearrange("p a b -> p (a b)"), bank(s.job)[:, :],
                                   ACT.Copy).then_inc(act_evac, 1)
                elif k == "o":
                    need(act, E_, dve_evac, jobs.evac[s.job])
                    need(act, E_, gla_sq, s.seq)
                    act.activation(junk_gla[:, :], o_gla[:, s.i, s.h * DV:(s.h + 1) * DV], ACT.Square,
                                   accum_out=gss[:, s.i, s.h:s.h + 1]).then_inc(gla_sq, 1)
                elif k == "gstat":
                    need(act, E_, gvar, 1)
                    act.activation(gstd[:, :, :], grstd[:, :, :], ACT.Sqrt).then_inc(gstd_done, 1)
                elif k == "mixT":
                    need(act, E_, mm, last_pb + 1)
                    need(act, E_, dve_evac, jobs.evac[last_pb])
                    act.activation(mT_hi[:, s.k, :], mixf[:, s.k, :], ACT.Copy).then_inc(mhi_done, 1)
                elif k == "norm2":
                    i = s.i
                    need(act, E_, dve_evac, jobs.evac[last_out] if i == NT - 1 else jobs.evac[find(kind="ts", dest=("out", 3), i=i)[0].job])
                    need(act, E_, sq2, i)
                    act.activation(junk2[:, :], x1[:, i, :], ACT.Square, accum_out=ss[:, i:i + 1]).then_inc(sq2, 1)
                    need(act, E_, var2, i + 1)
                    act.activation(std[:, i:i + 1], rstd[:, i:i + 1], ACT.Sqrt).then_inc(std2, 1)
                elif k == "h2T":
                    need(act, E_, mm, s.job + 1)
                    act.activation(h2T[:, s.i % 2, 4 * s.half:4 * s.half + 4, :],
                                   bank(s.job)[:, :].rearrange("p (k t) -> p k t", t=P), ACT.Copy).then_inc(act_evac, 1)
                elif k == "route":
                    need(act, E_, mm, last_out + 1)
                    need(act, E_, mlo_done, KD)
                    hi_weights("gate", 0, 0, 2, 0, 0)
                    hi_weights("up", 0, 0, 2, 0, 0)
                    need(act, E_, route_neg, 1)
                    act.activation(ex[:, :, :], ex[:, :, :], ACT.Exp).then_inc(route_exp, 1)
                    hi_weights("down", 0, 0, 2, 0, 0)
                    need(act, E_, route_neg2, 1)
                    act.activation(ratio[:, :], ratio[:, :], ACT.Exp).then_inc(route_exp2, 1)
                    for x in kinds:
                        hi_weights(x, 1, 1, 2, 1, 0)

            def hi_x(e, p, ring):
                act.wait_ge(xt_mm, e + 1)
                if not (isinstance(e, int) and e < ring):
                    act.wait_ge(gu_mm, e + (1 - ring))
                for half in range(2):
                    ins = act.activation(m_xT_hi[:, p, 4 * half:4 * half + 4, :],
                                         psum[B_XT[half]][:, :].rearrange("p (k t) -> p k t", t=P), ACT.Copy)
                ins.then_inc(xt_hi, 1)

            def silu(e, p, ring):
                act.wait_ge(gu_mm, e + 1)
                if not (isinstance(e, int) and e < ring):
                    act.wait_ge(a_done, e + (1 - ring))
                act.activation(m_sil[:, p, :], psum[B_GU[p]][:, 0:FF], ACT.Silu).then_inc(silu_done, 1)

            def hi_a(e, p, ring):
                act.wait_ge(at_mm, e + 1)
                if not (isinstance(e, int) and e < ring):
                    act.wait_ge(y_mm, e + (1 - ring))
                act.activation(m_aT_hi[:, p, :, :], psum[B_AT[p]][:, 0:2 * P].rearrange("p (k t) -> p k t", t=P), ACT.Copy)\
                   .then_inc(at_hi, 1)

            hi_x(0, 0, 2)
            hi_x(1, 1, 2)

            def tile(e, p, k, r, u):
                silu(e, p, 2)
                if ahead(e, 2):
                    hi_weights("gate", e + 2, p, 2, *later(r, u, 2))
                    hi_weights("up", e + 2, p, 2, *later(r, u, 2))
                hi_a(e, p, 2)
                if ahead(e, 2):
                    hi_x(e + 2, p, 2)
                if ahead(e, 1) and not first(e):
                    hi_weights("down", e + 1, 1 - p, 2, *later(r, u, 1))

            first_tiles(act.Fori, tile)

            def beyond_tile(e, j, k, u):
                for x in kinds:
                    hi_weights(x, e, 0, 1, 0, u)
                hi_x(e, 0, 1)
                silu(e, 0, 1)
                hi_a(e, 0, 1)

            beyond(act, beyond_tile)
            for i in range(NT):
                act.wait_ge(sum_done, i + 1)
                need(act, E_, sq3, i)
                act.activation(junk3[:, :], x1[:, i, :], ACT.Square, accum_out=ss[:, i:i + 1]).then_inc(sq3, 1)
                act.wait_ge(var3, i + 1)
                act.activation(std[:, i:i + 1], rstd[:, i:i + 1], ACT.Sqrt).then_inc(std3, 1)

        @block.tensor
        def _(pe):
            E_ = "pe"

            def claim(s):
                if s.job >= BANKS:
                    evac_done(pe, E_, s.job - BANKS)

            def product3(out, pairs):
                n = len(pairs)
                for j, (l_hi, l_lo, r_hi, r_lo) in enumerate(pairs):
                    pe.matmul(out, l_hi, r_hi, start=j == 0, stop=False)
                    pe.matmul(out, l_hi, r_lo, start=False, stop=False)
                    ins = pe.matmul(out, l_lo, r_hi, start=False, stop=j == n - 1)
                return ins

            for s in steps:
                k = s.kind
                if k in ("w", "norm", "comb", "decay", "gstat", "mixT", "norm2", "route", "place"):
                    continue
                claim(s)
                b_ = bank(s.job)
                if k == "vec":
                    need(pe, E_, rel_in, 32)
                    need(pe, E_, consts, 1)
                    ins = pe.matmul(b_[0:AH, :], relx[:, s.a * AH:(s.a + 1) * AH],
                                    onehot[:, s.a, s.half * 512:(s.half + 1) * 512], start=True, stop=True)
                elif k == "hT":
                    need(pe, E_, consts, 2)
                    need(pe, E_, xn_done, s.i + 1)
                    for c in range(4):
                        ins = pe.transpose(b_[:, c * P:(c + 1) * P],
                                           xin[:, s.i, (4 * s.half + c) * P:(4 * s.half + c + 1) * P], ident[:, :])
                elif k in ("ws", "ts"):
                    g, (name, a) = s.g, s.dest
                    kb, n = group_shape(g)
                    need(pe, E_, wlo_done, g + 1)
                    x_hi, x_lo = {"pa": (oaT_hi, oaT_lo), "pb": (obT_hi, obT_lo), "out": (mT_hi, mT_lo)}\
                        .get(name, (hT_hi, hT_lo))
                    if name == "pa":
                        evac_done(pe, E_, find(kind="oaT")[-1].job)
                    elif name == "pb":
                        evac_done(pe, E_, find(kind="obT")[-1].job)
                    elif name == "out":
                        need(pe, E_, mlo_done, KD)
                    else:
                        evac_done(pe, E_, last_hT)
                    if k == "ws":
                        m = min(P, n)
                        tok = slice(s.s * HALF, (s.s + 1) * HALF)
                        ins = product3(b_[0:m, 0:HALF],
                                       [(w_hi[:, g % 2, j, s.b * P:s.b * P + m], w_lo[:, g % 2, j, s.b * P:s.b * P + m],
                                         x_hi[:, j, tok], x_lo[:, j, tok]) for j in range(kb)])
                    else:
                        tok = slice(s.i * P, (s.i + 1) * P)
                        ins = product3(b_[:, 0:GW],
                                       [(x_hi[:, j, tok], x_lo[:, j, tok], w_hi[:, g % 2, j, :], w_lo[:, g % 2, j, :])
                                        for j in range(kb)])
                elif k == "sc":
                    u = s.u
                    evac_done(pe, E_, last_of_group[gnum["k", u.a]])
                    k0 = P * (u.i - 1) + CH + u.lo if u.a == 0 else u.first * P
                    for hh, h in enumerate(u.heads):
                        rows = slice(HD * (h % 2), HD * (h % 2) + HD)
                        ins = pe.matmul(b_[:, hh * u.width:(hh + 1) * u.width],
                                        qk[rows, u.a % 2, h // 2, u.i * P:(u.i + 1) * P],
                                        qk[rows, u.a % 2, 2 + h // 2, k0:k0 + u.width], start=True, stop=True)
                elif k == "pt":
                    u = s.u
                    need(pe, E_, probs, u.n + 1)
                    if u.a == 0:
                        need(pe, E_, pad_zero, 1)
                        src = [pad[:, u.n % 2, (t - u.i + 1) * P:(t - u.i + 2) * P] for t in u.ktiles]
                    else:
                        src = [sc[:, u.n % 3, (hh * len(u.ktiles) + j) * P:(hh * len(u.ktiles) + j + 1) * P]
                               for hh in range(len(u.heads)) for j in range(len(u.ktiles))]
                    for j, x in enumerate(src):
                        ins = pe.transpose(b_[:, j * P:(j + 1) * P], x, ident[:, :])
                elif k == "pv":
                    u = s.u
                    evac_done(pe, E_, u.pt)
                    evac_done(pe, E_, last_of_group[gnum["v", u.a]])
                    nk = len(u.ktiles)
                    for hh, h in enumerate(u.heads):
                        for j, t in enumerate(u.ktiles):
                            x = (hh * nk + j) * P
                            ins = pe.matmul(b_[:, hh * HD:(hh + 1) * HD], ptr[:, u.n % 3, x:x + P],
                                            va[:, u.a % 2, t, h * HD:(h + 1) * HD], start=j == 0, stop=j == nk - 1)
                elif k == "oaT":
                    need(pe, E_, oa_done, s.i + 1)
                    for c in range(2):
                        ins = pe.transpose(b_[:, c * P:(c + 1) * P], o_att[:, s.i, 0, c * P:(c + 1) * P], ident[:, :])
                elif k == "z":
                    need(pe, E_, wg_in, 32 * (s.h + 1))
                    evac_done(pe, E_, last_of_group[gnum["gate", 0]])
                    ins = pe.matmul(b_[:, 0:HALF], wgate[:, s.d, :], gT[:, s.s * HALF:(s.s + 1) * HALF],
                                    start=True, stop=True)
                elif k == "kot":
                    for j in range(4):
                        d, t = divmod(4 * s.q + j, NT)
                        need(pe, E_, ko, 2 * s.h + d + 1)
                        ins = pe.transpose(b_[:, j * P:(j + 1) * P], et[:, d, t * P:(t + 1) * P], ident[:, :])
                elif k == "state":
                    evac_done(pe, E_, find(kind="kot", h=s.h)[-1].job)
                    evac_done(pe, E_, last_of_group[gnum["vb", s.h]])
                    c = 2 * s.first + (s.t if s.d == 0 else s.nc - 1 - s.t)
                    rows = slice(CH * (c % 2), CH * (c % 2) + CH)
                    ins = pe.matmul(b_[:, 0:DV], kot[rows, s.d * NT + c // 2, :], vb[rows, c // 2, :],
                                    start=True, stop=True)
                elif k == "intra":
                    need(pe, E_, kin, 2 * s.h + 2)
                    tok = slice(s.i * P, (s.i + 1) * P)
                    for d in range(2):
                        ins = pe.matmul(b_[:, d * P:(d + 1) * P], k_in[:, d, tok], q_in[:, d, tok], start=True, stop=True)
                elif k == "o":
                    it = find(kind="intra", h=s.h, i=s.i)[0]
                    evac_done(pe, E_, it.job)
                    stt = find(kind="state", h=s.h, first=s.first)
                    evac_done(pe, E_, stt[-1].job)
                    nch = 2 * s.n
                    parts = []
                    for half in range(2):
                        c = 2 * (s.i - s.first) + half
                        tok = slice(s.i * P + half * CH, s.i * P + (half + 1) * CH)
                        if c > 0:
                            parts.append((half, q_in[:, 0, tok], st[:, 0, c - 1, :]))
                        if c < nch - 1:
                            parts.append((half, q_in[:, 1, tok], st[:, 1, nch - 2 - c, :]))
                    pe.matmul(b_[:, 0:DV], ptg[:, it.seq % 2, :], vb[:, s.i, :], start=True, stop=False,
                              skip_group_check=True)
                    for j, (half, l, r) in enumerate(parts):
                        ins = pe.matmul(b_[half * CH:(half + 1) * CH, 0:DV], l, r, start=False,
                                        stop=j == len(parts) - 1, skip_group_check=True)
                elif k == "obT":
                    need(pe, E_, ob_done, NT * s.h + s.i + 1)
                    for c in range(2):
                        x = s.h * DV + c * P
                        ins = pe.transpose(b_[:, c * P:(c + 1) * P], o_gla[:, s.i, x:x + P], ident[:, :])
                elif k == "h2T":
                    need(pe, E_, h2_done, s.i + 1)
                    for c in range(4):
                        ins = pe.transpose(b_[:, c * P:(c + 1) * P],
                                           h2[:, s.i, (4 * s.half + c) * P:(4 * s.half + c + 1) * P], ident[:, :])
                elif k == "router":
                    need(pe, E_, moe_in, 5 * 16)
                    evac_done(pe, E_, find(kind="h2T", i=s.i)[-1].job)
                    for j in range(KD):
                        ins = pe.matmul(b_[:, 0:NR], h2T[:, s.i % 2, j, :], wr[:, j, :], start=j == 0, stop=j == KD - 1)
                elif k == "rank":
                    need(pe, E_, hot_done, 1)
                    for i in range(NT):
                        for j in range(i + 1):
                            pe.matmul(b_[:, i * NE:(i + 1) * NE], (earlier if j == i else ones)[:, :], both[:, j, :],
                                      start=j == 0, stop=j == i)
                    for j in range(NT):
                        ins = pe.matmul(b_[:, NT * NE:(NT + 1) * NE], ones[:, :], both[:, j, :], start=j == 0, stop=j == NT - 1)
                elif k == "table":
                    need(pe, E_, place_done, 1)
                    for j in range(2 * NT):
                        ins = pe.matmul(b_[:, 0:SLOTS], row_hot[:, j, :], slot_hot[:, j, :], start=j == 0, stop=j == 2 * NT - 1)
                ins.then_inc(mm, 1)

            def xt(e, p, k):
                pe.wait_ge(x_gathered[p], k * 16 + 16)
                if not (isinstance(e, int) and e == 0):
                    pe.wait_ge(xt_lo, e)
                for c in range(KD):
                    ins = pe.transpose(psum[B_XT[c // 4]][:, (c % 4) * P:(c % 4 + 1) * P], m_x[:, p, c * P:(c + 1) * P],
                                       ident[:, :])
                ins.then_inc(xt_mm, 1)

            def gate_up(e, p, r, ring):
                pe.wait_ge(xt_lo, e + 1)
                if not (isinstance(e, int) and e < ring):
                    pe.wait_ge(a_done, e + (1 - ring))
                for n, x in enumerate(("gate", "up")):
                    pe.wait_ge(w_lo_done[x], e + 1)
                    ins = product3(psum[B_GU[p]][:, n * FF:(n + 1) * FF],
                                   [(m_xT_hi[:, p, j, :], m_xT_lo[:, p, j, :], m_hi[x][:, p, j, :], m_lo[x][:, r, j, :])
                                    for j in range(KD)])
                ins.then_inc(gu_mm, 1)

            def aT(e, p, ring):
                pe.wait_ge(a_done, e + 1)
                if not (isinstance(e, int) and e < ring):
                    pe.wait_ge(at_lo, e + (1 - ring))
                for c in range(2):
                    ins = pe.transpose(psum[B_AT[p]][:, c * P:(c + 1) * P], m_a[:, p, c * P:(c + 1) * P], ident[:, :])
                ins.then_inc(at_mm, 1)

            def down(e, p, r):
                pe.wait_ge(at_lo, e + 1)
                pe.wait_ge(w_lo_done["down"], e + 1)
                if not (isinstance(e, int) and e == 0):
                    pe.wait_ge(y_done, e)
                for half in range(2):
                    cols = slice(half * 512, (half + 1) * 512)
                    ins = product3(psum[B_Y[half]][:, :],
                                   [(m_aT_hi[:, p, j, :], m_aT_lo[:, p, j, :], m_hi["down"][:, p, j, cols],
                                     m_lo["down"][:, r, j, cols]) for j in range(2)])
                ins.then_inc(y_mm, 1)

            need(pe, E_, dve_evac, jobs.count["dve"])
            need(pe, E_, act_evac, jobs.count["act"])
            xt(0, 0, 0)
            xt(1, 1, 0)
            gate_up(0, 0, 0, 2)

            def tile(e, p, k, r, u):
                if ahead(e, 1):
                    gate_up(e + 1, 1 - p, later(r, u, 1)[0], 2)
                aT(e, p, 2)
                if ahead(e, 2):
                    xt(e + 2, p, k + 1)
                down(e, p, r)

            first_tiles(pe.Fori, tile)

            def beyond_tile(e, j, k, u):
                xt(e, 0, k)
                gate_up(e, 0, 0, 1)
                aT(e, 0, 1)
                down(e, 0, 0)

            beyond(pe, beyond_tile)

        @block.vector
        def _(dve):
            E_ = "dve"

            def mark(ins):
                counts["dve"] += 1
                ins.then_inc(dve_chain, 1)

            def settle():
                need(dve, E_, dve_chain, counts["dve"])

            def link(ins):
                mark(ins)
                settle()

            for s in steps:
                k = s.kind
                if k == "ts" and s.dest[0] == "og":
                    h, i = s.dest[1], s.i
                    x = o_gla[:, i, h * DV:(h + 1) * DV]
                    link(dve.scalar_tensor_tensor(x, x, grstd[:, i, h:h + 1], g_gla[:, :], ALU.mult, ALU.mult))
                    evac_done(dve, E_, s.job)
                    dve.tensor_tensor(x, x, sg[:, (NT * h + i) % 2, :], ALU.mult).then_inc(ob_done, 1)
                    continue
                if s.job is not None:
                    if jobs.by[s.job] != "dve":
                        continue
                    b_ = bank(s.job)
                if k == "norm":
                    i = s.i
                    need(dve, E_, sq_done, i + 1)
                    dve.tensor_scalar(rstd[:, i:i + 1], ss[:, i:i + 1], 1.0 / D, EPS, ALU.mult, ALU.add).then_inc(var_done, 1)
                    need(dve, E_, std_done, i + 1)
                    link(dve.reciprocal(rstd[:, i:i + 1], std[:, i:i + 1]))
                    need(dve, E_, gmix_in, 16)
                    dve.scalar_tensor_tensor(xin[:, i, :], xin[:, i, :], rstd[:, i:i + 1], g_mix[:, :],
                                             ALU.mult, ALU.mult).then_inc(xn_done, 1)
                elif k in ("hT", "oaT", "obT"):
                    need(dve, E_, hi_done, s.hi)
                    if k == "hT":
                        ks, lo, hi = slice(4 * s.half, 4 * s.half + 4), hT_lo, hT_hi
                    elif k == "oaT":
                        ks, lo, hi = slice(0, 2), oaT_lo, oaT_hi
                    else:
                        ks, lo, hi = slice(2 * s.h, 2 * s.h + 2), obT_lo, obT_hi
                    tok, n = slice(s.i * P, (s.i + 1) * P), (ks.stop - ks.start) * P
                    dve.tensor_tensor(lo[:, ks, tok], b_[:, 0:n].rearrange("p (k t) -> p k t", t=P),
                                      hi[:, ks, tok].bitcast(F32), ALU.subtract).then_inc(dve_evac, 1)
                elif k in ("ws", "ts"):
                    name, a = s.dest
                    need(dve, E_, mm, s.job + 1)
                    if name == "pa":
                        tok = slice(s.s * HALF, (s.s + 1) * HALF)
                        evac_done(dve, E_, last_of_group[gnum["ma", a]])
                        dve.tensor_tensor(sga[:, s.b, tok], sga[:, s.b, tok], b_[:, 0:HALF], ALU.mult).then_inc(dve_evac, 1)
                    elif name == "pb":
                        tok = slice(s.s * HALF, (s.s + 1) * HALF)
                        evac_done(dve, E_, last_of_group[gnum["mb", a]])
                        evac_done(dve, E_, last_of_group[gnum["pa", a]])
                        link(dve.tensor_tensor(sgb[:, s.b, tok], sgb[:, s.b, tok], b_[:, 0:HALF], ALU.mult))
                        dve.tensor_tensor(mixf[:, 2 * a + s.b, tok], sga[:, s.b, tok], sgb[:, s.b, tok],
                                          ALU.add).then_inc(dve_evac, 1)
                    else:
                        cols = slice(a * GW, (a + 1) * GW)
                        need(dve, E_, x1_in[s.i], 16)
                        dve.tensor_tensor(x1[:, s.i, cols], x1[:, s.i, cols], b_[:, 0:GW], ALU.add).then_inc(dve_evac, 1)
                elif k == "sc":
                    u = s.u
                    need(dve, E_, mm, s.job + 1)
                    need(dve, E_, table_in, 16 * NG)
                    if u.n >= 3:
                        need(dve, E_, mm, units[u.n - 3].pt + 1)
                    t0 = u.lo if u.a == 0 else 384 - P * u.t
                    for hh, h in enumerate(u.heads):
                        cols = slice(hh * u.width, (hh + 1) * u.width)
                        ins = dve.tensor_tensor_reduce(out=sc[:, u.n % 3, cols], in0=b_[:, cols],
                                                       in1=table[u.a][:, h, t0:t0 + u.width], scale=1.0, scalar=-3e38,
                                                       op0=ALU.add, op1=ALU.max, accum_out=mx[:, u.i, u.a, h:h + 1])
                    ins.then_inc(dve_evac, 1)
                    need(dve, E_, dve_evac, jobs.evac[s.job])
                    hs = slice(u.heads[0], u.heads[-1] + 1, 2)
                    dve.tensor_scalar(nmx[:, u.i, u.a, hs], mx[:, u.i, u.a, hs], -1.0, None,
                                      ALU.mult).then_inc(neg_max, 1)
                elif k == "pt":
                    u = s.u
                    n = len(u.heads) * len(u.ktiles) * P
                    need(dve, E_, mm, s.job + 1)
                    dve.tensor_copy(ptr[:, u.n % 3, 0:n], b_[:, 0:n]).then_inc(dve_evac, 1)
                elif k == "comb":
                    need(dve, E_, probs, NU)
                    link(dve.tensor_tensor(cm[:, :, :], mx[:, :, 0, :], mx[:, :, 1, :], ALU.max))
                    link(dve.tensor_tensor(cm[:, :, :], cm[:, :, :], mx[:, :, 2, :], ALU.max))
                    for a in range(NG):
                        ins = dve.tensor_tensor(mx[:, :, a, :], mx[:, :, a, :], cm[:, :, :], ALU.subtract)
                        if a < NG - 1:
                            mark(ins)
                    ins.then_inc(comb_neg, 1)
                    need(dve, E_, comb_exp, 1)
                    link(dve.tensor_tensor(wgrp[:, :, :, :], nmx[:, :, :, :], sm[:, :, :, :], ALU.mult))
                    link(dve.tensor_tensor(cden[:, :, :], wgrp[:, :, 0, :], wgrp[:, :, 1, :], ALU.add))
                    link(dve.tensor_tensor(cden[:, :, :], cden[:, :, :], wgrp[:, :, 2, :], ALU.add))
                    link(dve.reciprocal(cden[:, :, :], cden[:, :, :]))
                    for a in range(NG):
                        mark(dve.tensor_tensor(wgrp[:, :, a, :], nmx[:, :, a, :], cden[:, :, :], ALU.mult))
                    settle()
                    evac_done(dve, E_, units[-1].pv)
                    for i in range(NT):
                        for a in range(NG):
                            x = o_att[:, i, a, :].rearrange("p (h d) -> p h d", d=HD)
                            wv = wgrp[:, i, a, :].rearrange("p (h o) -> p h o", o=1).broadcast_to([P, AH, HD])
                            mark(dve.tensor_tensor(x, x, wv, ALU.mult))
                        settle()
                        link(dve.tensor_tensor(o_att[:, i, 0, :], o_att[:, i, 0, :], o_att[:, i, 1, :], ALU.add))
                        dve.tensor_tensor(o_att[:, i, 0, :], o_att[:, i, 0, :], o_att[:, i, 2, :], ALU.add).then_inc(oa_done, 1)
                elif k == "decay":
                    h = s.h
                    q, kk = qkb[h % 2][:, 0, :], qkb[h % 2][:, 1, :]
                    chunks = lambda x: x.rearrange("p (c t) -> p c t", t=CH)
                    for d in range(2):
                        need(dve, E_, softplus, 2 * h + d + 1)
                        mark(dve.scalar_tensor_tensor(zt[:, d, :], zt[:, d, :], 0.0, et[:, d, :], ALU.min, ALU.subtract))
                    settle()
                    for d in range(2):
                        x = zt[:, d, :] if d == 0 else zt[:, d, ::-1]
                        dve.tensor_tensor_scan(x, scan_mask[:, :], x, 0.0, ALU.mult, ALU.add).then_inc(cum, 1)
                    for d in range(2):
                        need(dve, E_, e1, 4 * h + 2 * d + 2)
                        evac_done(dve, E_, last_of_group[gnum["qkb", h]])
                        if h:
                            need(dve, E_, mm, find(kind="o", h=h - 1)[-1].job + 1)
                        dve.scalar_tensor_tensor(q_in[:, d, :], q, DK ** -0.5, et[:, d, :], ALU.mult, ALU.mult).then_inc(qin, 1)
                    for d in range(2):
                        need(dve, E_, e2, 2 * h + d + 1)
                        dve.tensor_tensor(k_in[:, d, :], kk, et[:, d, :], ALU.mult).then_inc(kin, 1)
                        need(dve, E_, kin, 2 * h + d + 1)
                        b = chunks(zt[:, d, :])
                        at_ = CH - 1 if d == 0 else 0
                        dve.tensor_tensor(chunks(et[:, d, :]), b[:, :, at_:at_ + 1].broadcast_to([P, NCH, CH]), b,
                                          ALU.subtract).then_inc(dd, 1)
                    for d in range(2):
                        need(dve, E_, e3, 2 * h + d + 1)
                        dve.tensor_tensor(et[:, d, :], kk, et[:, d, :], ALU.mult).then_inc(ko, 1)
                elif k == "state":
                    need(dve, E_, mm, s.job + 1)
                    c = 2 * s.first + (s.t if s.d == 0 else s.nc - 1 - s.t)
                    if s.t == 0:
                        dve.tensor_copy(st[:, s.d, 0, :], b_[:, 0:DV]).then_inc(dve_evac, 1)
                    else:
                        need(dve, E_, dve_evac, jobs.evac[s.prev])
                        dve.scalar_tensor_tensor(st[:, s.d, s.t, :], st[:, s.d, s.t - 1, :], dec[:, s.h % 2, s.d, c:c + 1],
                                                 b_[:, 0:DV], ALU.mult, ALU.add).then_inc(dve_evac, 1)
                elif k == "intra":
                    need(dve, E_, mm, s.job + 1)
                    p = ptg[:, s.seq % 2, :]
                    link(dve.copy_predicated(p, mask_f[:, :], b_[:, 0:P]))
                    dve.copy_predicated(p, mask_b[:, :], b_[:, P:2 * P]).then_inc(dve_evac, 1)
                elif k == "o":
                    need(dve, E_, mm, s.job + 1)
                    dve.tensor_copy(o_gla[:, s.i, s.h * DV:(s.h + 1) * DV], b_[:, 0:DV]).then_inc(dve_evac, 1)
                elif k == "gstat":
                    need(dve, E_, gla_sq, NT * GH)
                    dve.tensor_scalar(grstd[:, :, :], gss[:, :, :], 1.0 / DV, EPS, ALU.mult, ALU.add).then_inc(gvar, 1)
                    need(dve, E_, gstd_done, 1)
                    link(dve.reciprocal(grstd[:, :, :], gstd[:, :, :]))
                    need(dve, E_, ggla_in, 16)
                elif k == "norm2":
                    i = s.i
                    need(dve, E_, sq2, i + 1)
                    dve.tensor_scalar(rstd[:, i:i + 1], ss[:, i:i + 1], 1.0 / D, EPS, ALU.mult, ALU.add).then_inc(var2, 1)
                    need(dve, E_, std2, i + 1)
                    link(dve.reciprocal(rstd[:, i:i + 1], std[:, i:i + 1]))
                    need(dve, E_, moe_in, 5 * 16)
                    dve.scalar_tensor_tensor(h2[:, i, :], x1[:, i, :], rstd[:, i:i + 1], g_moe[:, :],
                                             ALU.mult, ALU.mult).then_inc(h2_done, 1)
                elif k == "router":
                    need(dve, E_, mm, s.job + 1)
                    need(dve, E_, moe_in, 5 * 16)
                    i = s.i
                    if i == 0:
                        link(dve.memset(l_grp[:, :, :], -3e38))
                    mark(dve.tensor_tensor(l_grp[:, i, 0:NGRP], b_[:, 0:NGRP], r_bias[:, 0:NGRP], ALU.add))
                    dve.tensor_tensor(l_exp[:, i, :], b_[:, NGRP:NR], r_bias[:, NGRP:NR], ALU.add).then_inc(dve_evac, 1)
                elif k == "route":
                    wide = lambda x, n: x.rearrange("p (i o) -> p i o", o=1).broadcast_to([P, NT, n])
                    settle()
                    need(dve, E_, dve_evac, jobs.evac[find(kind="router")[-1].job])
                    need(dve, E_, rconst, 1)
                    for i in range(NT):
                        mark(dve.max(top[:, i, :], l_grp[:, i, :]))
                    settle()
                    for i in range(NT):
                        mark(dve.max_index(top_at[:, i, :], top[:, i, :], l_grp[:, i, :]))
                    dve.tensor_tensor(ex[:, :, :], l_grp[:, :, :], top[:, :, 0:1].broadcast_to([P, NT, 8]),
                                      ALU.subtract).then_inc(route_neg, 1)
                    settle()
                    link(dve.tensor_copy(g_at[:, :], top_at[:, :, 0]))
                    for g in range(NGRP):
                        link(dve.tensor_scalar(p_grp[:, :], g_at[:, :], float(g), None, ALU.is_equal))
                        x = l_exp[:, :, g * EPG:(g + 1) * EPG]
                        if g == 0:
                            link(dve.tensor_tensor(l_sel[:, :, :], x, wide(p_grp[:, :], EPG), ALU.mult))
                        else:
                            link(dve.tensor_tensor(x, x, wide(p_grp[:, :], EPG), ALU.mult))
                            link(dve.tensor_tensor(l_sel[:, :, :], l_sel[:, :, :], x, ALU.add))
                    for i in range(NT):
                        mark(dve.max(top2[:, i, :], l_sel[:, i, :]))
                    settle()
                    for i in range(NT):
                        mark(dve.max_index(top2_at[:, i, :], top2[:, i, :], l_sel[:, i, :]))
                    dve.tensor_tensor(ratio[:, :], top2[:, :, 1], top2[:, :, 0], ALU.subtract).then_inc(route_neg2, 1)
                    settle()
                    link(dve.tensor_copy(e_at[:, :, :], top2_at[:, :, 0:2]))
                    for j in range(2):
                        link(dve.scalar_tensor_tensor(pos[:, :, j], g_at[:, :], float(EPG), e_at[:, :, j], ALU.mult, ALU.add))
                        it = iota_row[:, 0:NE].rearrange("p (o n) -> p o n", o=1).broadcast_to([P, NT, NE])
                        link(dve.tensor_tensor(hot[j][:, :, :], it, pos[:, :, j:j + 1].broadcast_to([P, NT, NE]), ALU.is_equal))
                    dve.tensor_tensor(both[:, :, :], hot[0][:, :, :], hot[1][:, :, :], ALU.add).then_inc(hot_done, 1)
                    need(dve, E_, route_exp, 1)
                    link(dve.tensor_reduce(p_grp[:, :], ex[:, :, :], AX.X, ALU.add))
                    link(dve.reciprocal(p_grp[:, :], p_grp[:, :]))
                    need(dve, E_, route_exp2, 1)
                    link(dve.tensor_scalar(g_at[:, :], ratio[:, :], 1.0, None, ALU.add))
                    link(dve.reciprocal(g_at[:, :], g_at[:, :]))
                    link(dve.tensor_tensor(pair_w[:, :, 0], g_at[:, :], p_grp[:, :], ALU.mult))
                    link(dve.tensor_tensor(pair_w[:, :, 1], pair_w[:, :, 0], ratio[:, :], ALU.mult))
                elif k == "rank":
                    need(dve, E_, mm, s.job + 1)
                    mark(dve.tensor_copy(rank[:, :, :], b_[:, 0:NT * NE].rearrange("p (i n) -> p i n", n=NE)))
                    dve.tensor_copy(tally[:, :], b_[:, NT * NE:(NT + 1) * NE]).then_inc(dve_evac, 1)
                elif k == "place":
                    settle()
                    need(dve, E_, dve_evac, jobs.evac[find(kind="rank")[0].job])
                    link(dve.tensor_scalar(n_over_e[:, :], tally[:, :], float(P), None, ALU.is_gt))
                    for m in range(2, T // P):
                        link(dve.scalar_tensor_tensor(n_over_e[:, :], tally[:, :], float(P * m), n_over_e[:, :],
                                                      ALU.is_gt, ALU.add))
                    link(dve.tensor_tensor_scan(over_end[:, :], ones[:, 0:NE], n_over_e[:, :], 0.0, ALU.mult, ALU.add))
                    link(dve.tensor_tensor(shift[:, :], over_end[:, :], n_over_e[:, :], ALU.subtract))
                    link(dve.tensor_tensor(shift[:, :], shift[:, :], iota_row[:, 0:NE], ALU.subtract))
                    link(dve.tensor_scalar(shift[:, :], shift[:, :], float(NE - 1), float(P), ALU.add, ALU.mult))
                    sh = shift[:, :].rearrange("p (o n) -> p o n", o=1).broadcast_to([P, NT, NE])
                    it = iota_row[:, 0:NE].rearrange("p (o n) -> p o n", o=1).broadcast_to([P, NT, NE])
                    link(dve.scalar_tensor_tensor(both[:, :, :], rank[:, :, :], float(P), sh, ALU.is_ge, ALU.mult))
                    link(dve.tensor_tensor(both[:, :, :], both[:, :, :], rank[:, :, :], ALU.add))
                    link(dve.scalar_tensor_tensor(both[:, :, :], it, float(P), both[:, :, :], ALU.mult, ALU.add))
                    for j in range(2):
                        link(dve.tensor_tensor(hot[j][:, :, :], hot[j][:, :, :], both[:, :, :], ALU.mult))
                        link(dve.tensor_reduce(pos[:, :, j], hot[j][:, :, :], AX.X, ALU.add))
                    link(dve.tensor_copy(pos_i[:, :, :], pos[:, :, :]))
                    mark(dve.tensor_copy(pair_idx[:, :, :], pos_i[:, :, :]))
                    link(dve.tensor_scalar(row_i[:, :, :], pos_i[:, :, :], P - 1, None, ALU.bitwise_and))
                    link(dve.tensor_copy(row_f[:, :, :], row_i[:, :, :]))
                    link(dve.tensor_tensor(slot_f[:, :, :], pos[:, :, :], row_f[:, :, :], ALU.subtract))
                    link(dve.tensor_scalar(slot_f[:, :, :], slot_f[:, :, :], 1.0 / P, None, ALU.mult))
                    need(dve, E_, h2_out, 16 * NT)
                    need(dve, E_, mm, find(kind="h2T")[-1].job + 1)
                    for i in range(NT):
                        for j in range(2):
                            mark(dve.tensor_scalar(row_hot[:, 2 * i + j, :], iota_row[:, :], row_f[:, i, j:j + 1], None, ALU.is_equal))
                            ins = dve.tensor_scalar(slot_hot[:, 2 * i + j, :], iota_row[:, 0:SLOTS], slot_f[:, i, j:j + 1],
                                                    iota_tok[:, i:i + 1], ALU.is_equal, ALU.mult)
                            if 2 * i + j < 2 * NT - 1:
                                mark(ins)
                    ins.then_inc(place_done, 1)
                    link(dve.tensor_tensor(over_cmp[:, :, :],
                                           over_end[0:1, :].rearrange("p (o n) -> p o n", o=1).broadcast_to([1, OVER, NE]),
                                           iota_row[0:1, 0:OVER].rearrange("p (n o) -> p n o", o=1).broadcast_to([1, OVER, NE]),
                                           ALU.is_le))
                    link(dve.tensor_reduce(over_f[:, 0:OVER], over_cmp[:, :, :], AX.X, ALU.add))
                    link(dve.tensor_scalar(over_f[:, 0:OVER], over_f[:, 0:OVER], float(NE - 1), None, ALU.min))
                    link(dve.tensor_copy(over_f[:, OVER:OVER + 1], over_end[0:1, NE - 1:NE]))
                    dve.tensor_copy(over_row[:, :], over_f[:, :]).then_inc(over_done, 1)
                elif k == "table":
                    need(dve, E_, mm, s.job + 1)
                    link(dve.tensor_scalar(tab0[:, :], b_[:, 0:SLOTS], 0.0, float(SKIP), ALU.is_equal, ALU.mult))
                    link(dve.scalar_tensor_tensor(tab[:, :], b_[:, 0:SLOTS], -1.0, tab0[:, :], ALU.add, ALU.add))
                    dve.tensor_copy(slot_idx[:, :], tab[:, :]).then_inc(dve_evac, 1)

            def lo_weights(x, e, p, r):
                dve.wait_ge(w_hi_done[x], e + 1)
                dve.tensor_tensor(m_lo[x][:, r], m_raw[x][:, r], m_hi[x][:, p].bitcast(F32),
                                  ALU.subtract).then_inc(w_lo_done[x], 1)

            def lo_x(e, p):
                dve.wait_ge(xt_hi, e + 1)
                for half in range(2):
                    ins = dve.tensor_tensor(m_xT_lo[:, p, 4 * half:4 * half + 4, :],
                                            psum[B_XT[half]][:, :].rearrange("p (k t) -> p k t", t=P),
                                            m_xT_hi[:, p, 4 * half:4 * half + 4, :].bitcast(F32), ALU.subtract)
                ins.then_inc(xt_lo, 1)

            def gated(e, p, ring):
                dve.wait_ge(silu_done, e + 1)
                if not (isinstance(e, int) and e < ring):
                    dve.wait_ge(at_mm, e + (1 - ring))
                dve.tensor_tensor(m_a[:, p, :], m_sil[:, p, :], psum[B_GU[p]][:, FF:2 * FF], ALU.mult).then_inc(a_done, 1)

            def lo_a(e, p):
                dve.wait_ge(at_hi, e + 1)
                dve.tensor_tensor(m_aT_lo[:, p, :, :], psum[B_AT[p]][:, 0:2 * P].rearrange("p (k t) -> p k t", t=P),
                                  m_aT_hi[:, p, :, :].bitcast(F32), ALU.subtract).then_inc(at_lo, 1)

            def result(e, p, k):
                dve.wait_ge(y_mm, e + 1)
                if not (isinstance(k, int) and k == 0):
                    dve.wait_ge(y_out[p], k * 16)
                for half in range(2):
                    ins = dve.tensor_copy(m_y[:, p, half * 512:(half + 1) * 512], psum[B_Y[half]][:, :])
                ins.then_inc(y_done, 1)

            lo_x(0, 0)
            lo_x(1, 1)
            for x in ("up", "down"):
                dve.wait_ge(w_lo_done[x], 2)

            def tile(e, p, k, r, u):
                gated(e, p, 2)
                if ahead(e, 2):
                    lo_weights("up", e + 2, p, later(r, u, 2)[0])
                lo_a(e, p)
                if ahead(e, 2):
                    lo_x(e + 2, p)
                if ahead(e, 1) and not first(e):
                    lo_weights("down", e + 1, 1 - p, later(r, u, 1)[0])
                result(e, p, k)

            first_tiles(dve.Fori, tile)

            def beyond_tile(e, j, k, u):
                for x in ("up", "down"):
                    lo_weights(x, e, 0, 0)
                lo_x(e, 0)
                gated(e, 0, 1)
                lo_a(e, 0)
                result(e, 0, k)

            beyond(dve, beyond_tile)
            for i in range(NT):
                dve.wait_ge(pair_in[i % 2], 32 * (i // 2 + 1))
                for j in range(2):
                    ins = dve.scalar_tensor_tensor(x1[:, i, :], y_pair[:, i % 2, j, :], pair_w[:, i, j:j + 1], x1[:, i, :],
                                                   ALU.mult, ALU.add)
                    if j == 0:
                        link(ins)
                ins.then_inc(sum_done, 1)
                dve.wait_ge(sq3, i + 1)
                dve.tensor_scalar(rstd[:, i:i + 1], ss[:, i:i + 1], 1.0 / D, EPS, ALU.mult, ALU.add).then_inc(var3, 1)
                dve.wait_ge(std3, i + 1)
                link(dve.reciprocal(rstd[:, i:i + 1], std[:, i:i + 1]))
                if i == 0:
                    dve.wait_ge(gfin_in, 16)
                if i >= 2:
                    dve.wait_ge(out_done[i % 2], 16 * (i // 2))
                dve.scalar_tensor_tensor(y_fin[:, i % 2, :], x1[:, i, :], rstd[:, i:i + 1], g_fin[:, :],
                                         ALU.mult, ALU.mult).then_inc(fin_done, 1)


def bucket_rows():
    import math
    import numpy as np

    rel = np.arange(VEC) - (S_PROMPT - 1)
    half_buckets, max_exact = NBK // 2, NBK // 4
    n = np.abs(rel)
    large = max_exact + (np.log(np.maximum(n, 1) / max_exact) / math.log(1024 / max_exact)
                         * (half_buckets - max_exact)).astype(np.int64)
    bucket = (rel > 0) * half_buckets + np.where(n < max_exact, n, np.minimum(large, half_buckets - 1))
    out = np.zeros((NBK + 1, NG, VEC), np.float32)
    for a, (win, dil) in enumerate(((128, 1), (512, 4), (2048, 16))):
        ok = (rel % dil == 0) & (n <= win // 2)
        for x in range(VEC):
            if ok[x]:
                out[bucket[x], a, x] = 1.0
            else:
                out[NBK, a, x] = NEG
    return out.reshape(NBK + 1, NG * VEC)


INPUTS = ["x_prompt", "x_sample", "norm_mix", "w_in", "rel_bias", "w_gate_f", "b_gate_f", "w_gate_b", "b_gate_b",
          "gla_norm", "w_proj_a", "w_proj_b", "w_out", "norm_moe", "w_router_group", "b_router_group",
          "w_router_expert", "b_router_expert", "w_exp_gate", "w_exp_up", "w_exp_down", "norm_final"]


def kernel(**inputs):
    import numpy as np
    import concourse.bacc as bacc
    from concourse.bass_utils import run_bass_kernel_spmd

    nc = bacc.Bacc("TRN2", target_bir_lowering=False, num_devices=1)
    arrays = {name: np.ascontiguousarray(inputs[name]) for name in INPUTS}
    arrays["const_buckets"] = bucket_rows()
    A = {name: nc.dram_tensor(f"in_{name}", a.shape, mybir.dt.from_np(a.dtype), kind="ExternalInput").ap()
         for name, a in arrays.items()}
    outs = [nc.dram_tensor(f"y_{name}", (1, rows, D), F32, kind="ExternalOutput").ap()
            for name, rows in (("prompt", S_PROMPT), ("sample", S_SAMPLE))]
    build(nc, A, outs)
    r = run_bass_kernel_spmd(nc, [{f"in_{name}": a for name, a in arrays.items()}], core_ids=[0])
    return r.results[0]["y_prompt"], r.results[0]["y_sample"]
```

```python
from contextlib import ExitStack

import concourse.bass as bass
from concourse import mybir

F32, F32R, I32, U32 = mybir.dt.float32, mybir.dt.float32r, mybir.dt.int32, mybir.dt.uint32
ALU = mybir.AluOpType
ACT = mybir.ActivationFunctionType
AX = mybir.AxisListType

P = 128
D = 1024
KD = D // P
S_PROMPT, S_SAMPLE = 512, 256
T = S_PROMPT + S_SAMPLE
NT = T // P
HALF = T // 2
SEQS = ((0, S_PROMPT // P), (S_PROMPT // P, S_SAMPLE // P))
NG = 3
AH = 4
HD = 64
AW = AH * HD
GH = 4
DK, DV = 128, 256
CH = 64
NCH = T // CH
RANK = 16
NE, NGRP, EPG, FF = 32, 4, 8, 256
NR = NGRP + NE
WRING = 3
OVER = 11
SLOTS = NE + OVER
EVEN = SLOTS + SLOTS % 2
NEG = -1e30
EPS = 1e-6
NBK = 32
VEC = 3 * P
NV = 1 + 2 * (NG - 1)
ROW = AW + 2 * AH
SKIP = 4096
C_QA, C_KA, C_VA = 0, 768, 1536
C_QB, C_KB, C_VB, C_OG = 2304, 2816, 3328, 4352
C_GATE = 5376
C_MA, C_MB = 5408, 6432
BANKS = 8
GW = 256


class Jobs:

    def __init__(self):
        self.by, self.count = [], {"act": 0, "dve": 0}
        self.evac = []

    def new(self, engine):
        self.by.append(engine)
        self.count[engine] += 1
        self.evac.append(self.count[engine])
        return len(self.by) - 1


class Step:

    def __init__(self, kind=None, a=None, b=None, d=None, dest=None, first=None, g=None, h=None, half=None,
                 heads=None, i=None, k=None, ktiles=None, lo=None, n=None, nc=None, q=None, s=None, t=None,
                 u=None, width=None):
        self.kind, self.a, self.b, self.d, self.dest, self.first, self.g = kind, a, b, d, dest, first, g
        self.h, self.half, self.heads, self.i, self.k, self.ktiles, self.lo = h, half, heads, i, k, ktiles, lo
        self.n, self.nc, self.q, self.s, self.t, self.u, self.width = n, nc, q, s, t, u, width
        self.job = self.sc = self.pt = self.pv = self.hi = self.prev = self.seq = None
        self.which = {"kind": kind, "a": a, "d": d, "dest": dest, "first": first, "h": h, "i": i, "s": s}


def interleave(a, b):
    out, j = [], 0
    for i, s in enumerate(a):
        out.append(s)
        while j < len(b) and (j + 1) * len(a) <= (i + 1) * len(b) + len(b) - 1 and j * len(a) < (i + 1) * len(b):
            out.append(b[j])
            j += 1
    return out + b[j:]


def plan():
    steps = []
    S = Step

    def groups():
        g = []
        for a in range(NG):
            g += [("q", a), ("k", a), ("v", a)]
        g += [("gate", 0)]
        for h in range(GH):
            g += [("qkb", h), ("vb", h)]
        g += [("og", h) for h in range(GH)]
        for m in range(4):
            g += [("ma", m), ("mb", m), ("pa", m), ("pb", m)]
        g += [("out", m) for m in range(4)]
        return g

    glist = groups()
    gnum = {g: n for n, g in enumerate(glist)}

    def proj(name, idx):
        n = gnum[name, idx]
        r = []
        if name in ("q", "k"):
            r = [S(kind="ws", g=n, b=b, s=s, dest=(name, idx)) for b in range(2) for s in range(2)]
        elif name == "gate":
            r = [S(kind="ws", g=n, b=0, s=s, dest=(name, idx)) for s in range(2)]
        elif name in ("qkb", "ma", "pa", "mb", "pb"):
            r = [S(kind="ws", g=n, b=b, s=s, dest=(name, idx)) for b in range(2) for s in range(2)]
        elif name in ("v", "vb", "og", "out"):
            r = [S(kind="ts", g=n, i=i, dest=(name, idx)) for i in range(NT)]
        if n + 2 < len(glist):
            r.append(S(kind="w", g=n + 2))
        return r

    for i in range(NT + 2):
        if i < NT:
            if i < NV:
                steps.append(S(kind="vec", a=i))
            steps.append(S(kind="norm", i=i))
        if i == NT:
            steps.append(S(kind="w", g=0))
        if i >= 2:
            steps += [S(kind="hT", i=i - 2, half=h) for h in range(2)]
    steps.append(S(kind="w", g=1))
    steps += proj("q", 0) + proj("k", 0) + proj("v", 0)

    def units(a):
        u = []
        for first, n in SEQS:
            for t in range(n):
                i = first + t
                if a == 0:
                    lo, hi = (P // 2 if t == 0 else 0), (3 * P // 2 if t == n - 1 else 2 * P)
                    ktiles = [x for x in (i - 1, i, i + 1) if first <= x < first + n]
                    u += [S(a=a, i=i, heads=[h], lo=lo, width=hi - lo, ktiles=ktiles, first=first) for h in range(AH)]
                else:
                    u += [S(a=a, i=i, heads=[h, h + 2], lo=0, width=P, ktiles=[i], first=i) for h in range(2)]
        return u

    allu = [units(a) for a in range(NG)]
    flat = [u for x in allu for u in x]
    for n, u in enumerate(flat):
        u.n = n
    for a in range(NG):
        r = []
        us = allu[a]
        for k in range(len(us) + 2):
            if k < len(us):
                r.append(S(kind="sc", u=us[k]))
            if 1 <= k <= len(us):
                r.append(S(kind="pt", u=us[k - 1]))
            if k >= 2:
                r.append(S(kind="pv", u=us[k - 2]))
                if a and (k == len(us) + 1 or us[k - 1].i != us[k - 2].i):
                    r.append(S(kind="natural", a=a, i=us[k - 2].i))
        if a + 1 < NG:
            other = proj("q", a + 1) + proj("k", a + 1) + proj("v", a + 1)
        else:
            other = proj("gate", 0) + proj("qkb", 0)
        steps += interleave(r, other)
    v = proj("vb", 0)
    z = [S(kind="z", h=0, d=d, s=s) for d in range(2) for s in range(2)]
    other = v[3:] + z
    steps += v[0:3] + [S(kind="comb")]
    for i in range(NT + 2):
        if i < NT:
            steps.append(S(kind="mix", i=i))
        if i >= 2:
            steps.append(S(kind="oaT", i=i - 2))
        steps += other[i:i + 1]

    def chain(h):
        r = [S(kind="z", h=h, d=d, s=s) for d in range(2) for s in range(2)] if h else []
        return r + [S(kind="decay", h=h)]

    def heavy(h):
        r = [S(kind="kot", h=h, q=q) for q in range(3)]
        for first, n in SEQS:
            nc_ = 2 * n
            r += [S(kind="state", h=h, first=first, nc=nc_, t=t, d=d) for t in range(nc_ - 1) for d in range(2)]
            for t in range(n + 1):
                if t < n:
                    r.append(S(kind="intra", h=h, i=first + t, first=first, n=n))
                if t:
                    r.append(S(kind="o", h=h, i=first + t - 1, first=first, n=n))
        return r

    for h in range(GH):
        steps += chain(h)
        if h:
            steps += proj("vb", h)
        if h + 1 < GH:
            steps += proj("qkb", h + 1)
        steps += heavy(h)
    steps.append(S(kind="gstat"))
    for h in range(GH):
        r = proj("og", h)
        steps += r[:NT] + [S(kind="obT", h=h, i=i) for i in range(NT)] + r[NT:]
    for m in range(4):
        for name in ("ma", "mb", "pa", "pb"):
            steps += proj(name, m)
            if m == 3 and name == "mb":
                steps += [S(kind="mixT", k=k) for k in range(KD - 2)]
    steps += [S(kind="mixT", k=k) for k in range(KD - 2, KD)]
    for m in range(3):
        steps += proj("out", m)
    r = proj("out", 3)
    for i in range(NT + 2):
        if i >= 2:
            steps += [S(kind="h2T", i=i - 2, half=h) for h in range(2)]
        if i < NT:
            steps += [r[i], S(kind="norm2", i=i)]
        if i >= 2:
            steps.append(S(kind="router", i=i - 2))
    steps += [S(kind="route"), S(kind="rank"), S(kind="place"), S(kind="table")]

    jobs = Jobs()
    act_evacuates = {"q", "k", "v", "gate", "qkb", "vb", "og", "ma", "mb"}
    last_of_group = {}
    for s in steps:
        if s.kind in ("ws", "ts"):
            s.job = jobs.new("act" if s.dest[0] in act_evacuates else "dve")
            last_of_group[s.g] = s.job
        elif s.kind in ("vec", "pv", "z", "kot", "h2T"):
            s.job = jobs.new("act")
        elif s.kind in ("hT", "sc", "oaT", "state", "intra", "o", "obT", "router", "rank", "table"):
            s.job = jobs.new("dve")
        elif s.kind == "pt":
            s.job = jobs.new("act" if s.u.n % 2 else "dve")
        if s.kind == "sc":
            s.u.sc = s.job
        elif s.kind == "pt":
            s.u.pt = s.job
        elif s.kind == "pv":
            s.u.pv = s.job
    n = 0
    for s in steps:
        if s.kind in ("hT", "oaT", "obT"):
            n += 1
            s.hi = n
    prev = {}
    for s in steps:
        if s.kind == "state":
            s.prev = prev.get(s.d)
            prev[s.d] = s.job
    for n, s in enumerate([s for s in steps if s.kind == "o"]):
        s.seq = n
    for n, s in enumerate([s for s in steps if s.kind == "intra"]):
        s.seq = n
    return steps, glist, gnum, flat, jobs, last_of_group


def build(nc, A, outs):
    steps, glist, gnum, units, jobs, last_of_group = plan()
    find = lambda **kw: [s for s in steps if all(s.which[k] == v for k, v in kw.items())]
    last_hT = find(kind="hT")[-1].job
    last_pb = last_of_group[gnum["pb", 3]]
    last_out = last_of_group[gnum["out", 3]]
    ctx = ExitStack()
    with ctx:
        BASE = 16512
        KB = 1024

        def at(name, shape, dtype, kb):
            off = BASE + int(kb * KB)
            size = 4
            for x in shape[1:]:
                size *= x
            assert off + size <= 229344, (name, off + size)
            return nc.alloc_sbuf_tensor_at(name, shape, dtype, offset=off)

        small = [0]

        def const(name, shape, dtype=F32):
            t = at(name, shape, dtype, small[0] / KB)
            size = 4
            for x in shape[1:]:
                size *= x
            small[0] += -(-size // 32) * 32
            assert small[0] <= 8 * KB, small[0]
            return t

        ident = const("ident", [P, P])
        mask_f = const("mask_f", [P, P], I32)
        mask_b = const("mask_b", [P, P], I32)
        scan_mask = const("scan_mask", [P, T])
        gate_bias = const("gate_bias", [P, 2, GH])
        eps = const("eps", [P, 1])
        zeros = const("zeros", [P, P])
        ss = const("ss", [P, NT])
        std = const("std", [P, NT])
        rstd = const("rstd", [P, NT])
        nmx = const("nmx", [P, NT, NG, AH])
        wgrp = const("wgrp", [P, NT, NG, AH])
        cm = const("cm", [P, NT, AH])
        cden = const("cden", [P, NT, AH])
        gss = const("gss", [P, NT, GH])
        gstd = const("gstd", [P, NT, GH])
        grstd = const("grstd", [P, NT, GH])
        junk_gla = const("junk_gla", [P, DV])
        dec = const("dec", [P, 2, 2, NCH])

        hT_hi = at("hT_hi", [P, KD, T], F32R, 8)
        hT_lo = at("hT_lo", [P, KD, T], F32R, 32)
        raw = at("raw", [P, 2, KD, GW], F32, 56)
        w_hi = at("w_hi", [P, 2, KD, GW], F32R, 72)
        w_lo = at("w_lo", [P, 2, KD, GW], F32R, 88)
        table = [at("table0", [P, AH, 2 * P], F32, 132), at("table1", [P, 2, AH, P], F32, 104),
                 at("table2", [P, 2, AH, P], F32, 114)]
        onehot = at("onehot", [NBK + 1, NV, VEC], F32, 118)
        vecs = at("vecs", [AH, NV, VEC], F32, 148)
        relx = at("relx", [NBK + 1, NG * AH], F32, 131.5)
        xin = at("xin", [P, NT, D], F32, 172)
        g_mix = at("g_mix", [P, D], F32, 196)
        junk = at("junk", [P, D], F32, 200)
        qk = at("qk", [P, 2, 4, T], F32, 136)
        va = at("va", [P, 2, NT, AW], F32, 160)
        o_att = at("o_att", [P, NT, NG, ROW], F32, 172)
        pad = at("pad", [P, 2, 3 * P], F32, 110)
        sc = at("sc", [P, 3, 512], F32, 193)
        ptr = at("ptr", [P, 3, 512], F32, 199)
        oaT_hi = at("oaT_hi", [P, 2, T], F32R, 104)
        oaT_lo = at("oaT_lo", [P, 2, T], F32R, 110)
        o_gla = at("o_gla", [P, NT, D], F32, 116)
        qkb = [at("qkb0", [P, 2, T], F32, 148), at("qkb1", [P, 2, T], F32, 140)]
        vb = at("vb", [P, NT, DV], F32, 154)
        ptg = at("ptg", [P, 2, P], F32, 146)
        wgate = at("wgate", [2 * RANK, 2, P], F32, 147)
        zt = at("zt", [P, 2, T], F32, 160)
        gT = at("gT", [2 * RANK, T], F32, 166)
        et = at("et", [P, 2, T], F32, 169)
        q_in = at("q_in", [P, 2, T], F32, 175)
        k_in = at("k_in", [P, 2, T], F32, 181)
        kot = at("kot", [P, 12, P], F32, 187)
        st = at("st", [P, 2, 7, DV], F32, 193)
        obT_hi = at("obT_hi", [P, KD, T], F32R, 140)
        obT_lo = at("obT_lo", [P, KD, T], F32R, 164)
        sg = at("sg", [P, 2, DV], F32, 188)
        g_gla = at("g_gla", [P, DV], F32, 190)
        sga = at("sga", [P, 2, T], F32, 191)
        sgb = at("sgb", [P, 2, T], F32, 197)
        mixf = at("mixf", [P, KD, T], F32, 116)
        mT_hi = at("mT_hi", [P, KD, T], F32R, 8)
        mT_lo = at("mT_lo", [P, KD, T], F32R, 32)
        x1 = at("x1", [P, NT, D], F32, 140)
        junk2 = at("junk2", [P, D], F32, 164)
        h2 = at("h2", [P, NT, D], F32, 168)
        g_moe = at("g_moe", [P, D], F32, 192)
        h2T = at("h2T", [P, 2, KD, P], F32, 196)
        wr = at("wr", [P, KD, NR], F32, 204)
        r_bias = at("r_bias", [P, NR], F32, 205.5)

        route_kb = [136.0]

        def route(name, shape, dtype=F32):
            t = at(name, shape, dtype, route_kb[0])
            size = 4
            for x in shape[1:]:
                size *= x
            route_kb[0] += -(-size // 32) * 32 / KB
            return t

        earlier = route("earlier", [P, P])
        ones = route("ones", [P, P])
        iota_row = route("iota_row", [P, P])
        iota_tok = route("iota_tok", [P, NT])
        l_grp = route("l_grp", [P, NT, 8])
        l_exp = route("l_exp", [P, NT, NE])
        slot_idx = route("slot_idx", [P, SLOTS], I32)
        pair_idx = route("pair_idx", [P, NT, 2], I32)
        pair_w = route("pair_w", [P, NT, 2])
        over_row = route("over_row", [1, OVER + 1], I32)
        x_idx = route("x_idx", [P, 2], I32)
        assert route_kb[0] <= 140
        route_kb[0] = 196.0
        top = route("top", [P, NT, 8])
        top_at = route("top_at", [P, NT, 8], U32)
        top2 = route("top2", [P, NT, 8])
        top2_at = route("top2_at", [P, NT, 8], U32)
        g_at = route("g_at", [P, NT])
        e_at = route("e_at", [P, NT, 2])
        p_grp = route("p_grp", [P, NT])
        ratio = route("ratio", [P, NT])
        ex = route("ex", [P, NT, 8])
        sel = route("sel", [P, NT, NGRP])
        hot = [route("hot0", [P, NT, NE]), route("hot1", [P, NT, NE])]
        both = route("both", [P, NT, NE])
        before = route("before", [P, NT + 1, NE])
        rank = route("rank", [P, NT, NE])
        tally = route("tally", [P, NE])
        n_over_e = route("n_over_e", [P, NE])
        over_end = route("over_end", [P, NE])
        shift = route("shift", [P, NE])
        pos = route("pos", [P, NT, 2])
        pos_i = route("pos_i", [P, NT, 2], I32)
        row_i = route("row_i", [P, NT, 2], I32)
        row_f = route("row_f", [P, NT, 2])
        slot_f = route("slot_f", [P, NT, 2])
        tab = route("tab", [P, SLOTS])
        tab0 = route("tab0", [P, SLOTS])
        over_cmp = route("over_cmp", [1, OVER, NE])
        over_f = route("over_f", [1, OVER + 1])
        assert route_kb[0] <= 203.8125, route_kb
        row_hot = at("row_hot", [P, 2 * NT, P], F32R, 172)
        slot_hot = at("slot_hot", [P, 2 * NT, EVEN], F32R, 178)
        slot_is = at("slot_is", [P, 2 * NT, EVEN], F32, 181)
        kinds = ("gate", "up", "down")
        m_raw, m_hi, m_lo = {}, {}, {}
        for n, x in enumerate(kinds):
            shape = [2, D] if x == "down" else [KD, FF]
            m_raw[x] = at(f"raw_{x}", [P, WRING] + shape, F32, 8 + 24 * n)
            m_lo[x] = at(f"lo_{x}", [P, WRING] + shape, F32R, 8 + 24 * n)
            m_hi[x] = at(f"hi_{x}", [P, 2] + shape, F32R, 80 + 16 * n)
        m_x = at("m_x", [P, 2, D], F32, 128)
        m_y = at("m_y", [P, 2, D], F32, 164)
        m_xT_hi = at("m_xT_hi", [P, 2, KD, P], F32R, 172)
        m_xT_lo = at("m_xT_lo", [P, 2, KD, P], F32R, 180)
        m_a = at("m_a", [P, 2, FF], F32, 188)
        m_sil = at("m_sil", [P, 2, FF], F32, 190)
        m_aT_hi = at("m_aT_hi", [P, 2, 2, P], F32R, 192)
        m_aT_lo = at("m_aT_lo", [P, 2, 2, P], F32R, 194)
        g_fin = at("g_fin", [P, D], F32, 203.8125)
        y_pair = at("y_pair", [P, NT, 2, D], F32, 8)
        y_fin = at("y_fin", [P, NT, D], F32, 56)
        junk3 = at("junk3", [P, D], F32, 80)

        psum = [ctx.enter_context(nc.psum_tensor(f"bank{b}", [P, 512], F32)) for b in range(BANKS)]
        bank = lambda job: psum[job % BANKS]

        vec_d = nc.dram_tensor("vec_d", (NV * AH, VEC), F32, kind="Internal").ap()
        rep_d = nc.dram_tensor("rep_d", (NV * AH * P, VEC), F32, kind="Internal").ap()
        att_d = nc.dram_tensor("att_d", (2 * T, ROW), F32, kind="Internal").ap()
        h2_d = nc.dram_tensor("h2_d", (T, D), F32, kind="Internal").ap()
        y_d = nc.dram_tensor("y_d", (SLOTS * P, D), F32, kind="Internal").ap()

        def sem(name):
            return ctx.enter_context(nc.semaphore(name))

        x_in = [sem(f"x_in{i}") for i in range(NT)]
        rel_in, gmix_in, bias_in, ggla_in, moe_in = (
            sem("rel_in"), sem("gmix_in"), sem("bias_in"), sem("ggla_in"), sem("moe_in"))
        raw_in = [sem("raw_in0"), sem("raw_in1")]
        wg_in = sem("wg_in")
        vec_out, rep_out, table_in = sem("vec_out"), sem("rep_out"), sem("table_in")
        consts = sem("consts")
        mm = sem("mm")
        act_evac, dve_evac = sem("act_evac"), sem("dve_evac")
        whi_done, wlo_done = sem("whi_done"), sem("wlo_done")
        hi_done = sem("hi_done")
        sq_done, var_done, std_done, xn_done = sem("sq_done"), sem("var_done"), sem("std_done"), sem("xn_done")
        att_out, att_in = ([sem(f"att_out{a}") for a in (1, 2)], [sem(f"att_in{a}") for a in (1, 2)])
        pad_zero, neg_max, probs = sem("pad_zero"), sem("neg_max"), sem("probs")
        comb_neg, comb_exp, oa_done = sem("comb_neg"), sem("comb_exp"), sem("oa_done")
        softplus, cum, e1, qin, e2, kin, e3, ko = (sem(x) for x in ("softplus", "cum", "e1", "qin", "e2", "kin", "e3", "ko"))
        dd = sem("dd")
        gla_sq, gvar, gstd_done, ob_done = sem("gla_sq"), sem("gvar"), sem("gstd_done"), sem("ob_done")
        mhi_done, mlo_done = sem("mhi_done"), sem("mlo_done")
        x1_in = [sem(f"x1_in{i}") for i in range(NT)]
        sq2, var2, std2, h2_done, h2_out = sem("sq2"), sem("var2"), sem("std2"), sem("h2_done"), sem("h2_out")
        act_chain, dve_chain, pool_chain = sem("act_chain"), sem("dve_chain"), sem("pool_chain")
        rconst, route_neg, route_exp, route_neg2, route_exp2 = (
            sem("rconst"), sem("route_neg"), sem("route_exp"), sem("route_neg2"), sem("route_exp2"))
        hot_done, place_done, over_done = sem("hot_done"), sem("place_done"), sem("over_done")
        w_arrived = {x: [sem(f"arrived_{x}{r}") for r in range(WRING)] for x in kinds}
        w_hi_done = {x: sem(f"hi_{x}_done") for x in kinds}
        w_lo_done = {x: sem(f"lo_{x}_done") for x in kinds}
        x_copied, x_gathered = sem("x_copied"), [sem("x_gathered0"), sem("x_gathered1")]
        xt_mm, xt_hi, xt_lo = sem("xt_mm"), sem("xt_hi"), sem("xt_lo")
        gu_mm, silu_done, a_done = sem("gu_mm"), sem("silu_done"), sem("a_done")
        at_mm, at_hi, at_lo = sem("at_mm"), sem("at_hi"), sem("at_lo")
        y_mm, y_done = sem("y_mm"), sem("y_done")
        y_out = [sem("y_out0"), sem("y_out1")]
        results_in, zero_out = sem("results_in"), sem("zero_out")
        gfin_in = sem("gfin_in")
        pair_in = [sem(f"pair_in{i}") for i in range(NT)]
        sum_done, sq3, std3, fin_done = sem("sum_done"), sem("sq3"), sem("std3"), sem("fin_done")
        out_done = sem("out_done")

        B_XT, B_GU, B_AT, B_Y = (0, 1), (2, 3), (4, 7), (5, 6)

        LOOPED = 4
        FIRST, TURN = 2, 2 * WRING

        def first_tiles(eng_fori, body):
            def one(e):
                body(e, e % 2, e // 2, e % WRING, e // WRING)

            for e in range(FIRST):
                one(e)
            with eng_fori(0, LOOPED) as turn:
                for c in range(FIRST, FIRST + TURN):
                    body(turn * TURN + c, c % 2, turn * WRING + c // 2, c % WRING, turn * 2 + c // WRING)
            for e in range(FIRST + LOOPED * TURN, NE):
                one(e)

        def later(r, u, n):
            return (r + n) % WRING, u + (r + n) // WRING

        def ahead(e, n):
            return not isinstance(e, int) or e + n < NE

        def first(e):
            return isinstance(e, int) and e == 0

        def beyond(eng, body):
            eng.wait_ge(over_done, 1)
            n_over = eng.value_load(over_row[0:1, OVER:OVER + 1], min_val=0, max_val=OVER)
            with eng.Fori(0, OVER) as j:
                with eng.If(n_over > j):
                    body(j + NE, j, j + NE // 2, j + (NE - 1) // WRING + 1)
            return n_over

        seen = {}

        def need(who, eng, s, value):
            if seen.get((eng, s.name), 0) < value:
                seen[eng, s.name] = value
                who.wait_ge(s, value)

        counts = {"act": 0, "dve": 0, "pool": 0}

        def evac_done(who, eng, job):
            by = jobs.by[job]
            need(who, eng, act_evac if by == "act" else dve_evac, jobs.evac[job])

        MAX, SUM = slice(AW, AW + AH), slice(AW + AH, ROW)

        def by_class(dst, src, half):
            parts = []
            for first, n in SEQS:
                lo, hi = max(first * P, half * HALF), min((first + n) * P, (half + 1) * HALF)
                if lo < hi:
                    u0, cnt = (lo - first * P) // n, (hi - lo) // n
                    d = dst[:, first * P:(first + n) * P].rearrange("p (r u) -> p r u", r=n)
                    parts.append((d[:, :, u0:u0 + cnt],
                                  src[:, lo - half * HALF:hi - half * HALF].rearrange("p (u r) -> p r u", r=n)))
            return parts

        def x_rows(i):
            if i < S_PROMPT // P:
                return A["x_prompt"][0, i * P:(i + 1) * P, :]
            i -= S_PROMPT // P
            return A["x_sample"][0, i * P:(i + 1) * P, :]

        def bcast(ap1d, n):
            return bass.AP(ap1d.tensor, ap1d.offset, [[0, P], [1, n]])

        def group_parts(g):
            name, a = glist[g]
            w_in = A["w_in"][0]
            cols = {"q": C_QA, "k": C_KA, "v": C_VA, "vb": C_VB, "og": C_OG, "ma": C_MA, "mb": C_MB}
            if name in cols:
                return [(w_in[:, cols[name] + GW * a:cols[name] + GW * (a + 1)], KD, 0, GW)]
            if name == "gate":
                return [(w_in[:, C_GATE:C_GATE + 2 * RANK], KD, 0, 2 * RANK)]
            if name == "qkb":
                return [(w_in[:, C_QB + DK * a:C_QB + DK * (a + 1)], KD, 0, DK),
                        (w_in[:, C_KB + DK * a:C_KB + DK * (a + 1)], KD, DK, DK)]
            src = {"pa": A["w_proj_a"], "pb": A["w_proj_b"], "out": A["w_out"]}[name][0]
            return [(src[:, GW * a:GW * (a + 1)], 2 if name == "pa" else KD, 0, GW)]

        raw_value = {}
        total = [0, 0]
        for g in range(len(glist)):
            total[g % 2] += 16 * len(group_parts(g))
            raw_value[g] = total[g % 2]

        def group_shape(g):
            name, _ = glist[g]
            return (2 if name == "pa" else KD), (2 * RANK if name == "gate" else GW)

        ZERO_FROM = gnum["vb", 0]
        assert ZERO_FROM + OVER < len(glist)

        def dve_splits(g):
            return g == 0 or glist[g - 1][0] == "pa"

        block = ctx.enter_context(nc.Block())

        @block.sync
        def _(sp):
            E_ = "sp"
            sp.dma_start(onehot[:, :, :], A["const_buckets"].rearrange("b (a n) -> b a n", a=NV)).then_inc(rel_in, 16)
            sp.dma_start(relx[0:NBK, :], A["rel_bias"]).then_inc(rel_in, 16)
            sp.dma_start(xin[:, 0, :], x_rows(0)).then_inc(x_in[0], 16)
            sp.dma_start(g_mix[:, :], bcast(A["norm_mix"], D)).then_inc(gmix_in, 16)
            for i in range(1, NT):
                sp.dma_start(xin[:, i, :], x_rows(i)).then_inc(x_in[i], 16)

            def replicate_vectors():
                need(sp, E_, act_evac, jobs.evac[find(kind="vec")[-1].job])
                sp.dma_start(vec_d.rearrange("(a h) n -> h a n", a=NV), vecs[:, :, :]).then_inc(vec_out, 16)
                sp.wait_ge(vec_out, 16)
                sp.dma_start(bass.AP(rep_d.tensor, 0, [[P * VEC, NV * AH], [VEC, P], [1, VEC]]),
                             bass.AP(vec_d.tensor, 0, [[VEC, NV * AH], [0, P], [1, VEC]])).then_inc(rep_out, 16)

            def bias_tables():
                sp.wait_ge(rep_out, 16)
                for v in range(NV):
                    out, width = (table[0][:, :, :], 2 * P) if v == 0 else (table[1 + (v - 1) // 2][:, (v - 1) % 2, :, :], P)
                    sp.dma_start(out, bass.AP(rep_d.tensor, v * AH * P * VEC + P - 1,
                                              [[VEC - 1, P], [P * VEC, AH], [1, width]])).then_inc(table_in, 16)
                for d, name in enumerate(("b_gate_f", "b_gate_b")):
                    sp.dma_start(gate_bias[:, d, :], A[name][0].rearrange("(h p) -> p h", p=P),
                                 allow_slow_non_contiguous=True).then_inc(bias_in, 16)

            for s in steps:
                if s.kind == "w":
                    for g in (0, 1) if s.g == 0 else (s.g + 1,) if s.g + 1 < len(glist) else ():
                        if g >= 2:
                            need(sp, E_, wlo_done, g - 1)
                        for src, kb, c0, n in group_parts(g):
                            sp.dma_start(raw[:, g % 2, 0:kb, c0:c0 + n],
                                         src.rearrange("(k p) n -> p k n", p=P)).then_inc(raw_in[g % 2], 16)
                    if s.g == 0:
                        replicate_vectors()
                    elif s.g == 2:
                        bias_tables()
                    elif ZERO_FROM <= s.g < ZERO_FROM + OVER:
                        need(sp, E_, consts, 2)
                        x = NE + s.g - ZERO_FROM
                        sp.dma_start(y_d[x * P:(x + 1) * P, :].rearrange("p (c n) -> p c n", n=P),
                                     zeros[:, :].rearrange("p (a n) -> p a n", a=1)
                                     .broadcast_to([P, KD, P])).then_inc(zero_out, 16)
                if s.kind == "natural":
                    a = s.a
                    last = [u for u in units if u.a == a and u.i == s.i][-1]
                    need(sp, E_, probs, last.n + 1)
                    evac_done(sp, E_, last.pv)
                    first, n = SEQS[0] if s.i < SEQS[1][0] else SEQS[1]
                    row = (a - 1) * T + first * P + s.i - first
                    sp.dma_start(bass.AP(att_d.tensor, row * ROW, [[n * ROW, P], [1, ROW]]),
                                 o_att[:, s.i, a, :]).then_inc(att_out[a - 1], 16)
                    back = {(2, 0): 1, (2, NT - 1): 2}.get((a, s.i))
                    if back:
                        sp.wait_ge(att_out[back - 1], 16 * NT)
                        sp.dma_start(o_att[:, :, back, :],
                                     bass.AP(att_d.tensor, (back - 1) * T * ROW, [[ROW, P], [P * ROW, NT], [1, ROW]]))\
                          .then_inc(att_in[back - 1], 16)
                if s.kind == "ts" and s.dest == ("out", 0) and s.i == 0:
                    evac_done(sp, E_, last_pb)
                    for i in range(NT):
                        sp.dma_start(x1[:, i, :], x_rows(i)).then_inc(x1_in[i], 16)
                    sp.dma_start(g_moe[:, :], bcast(A["norm_moe"], D)).then_inc(moe_in, 16)
                    sp.dma_start(wr[:, :, 0:NGRP], A["w_router_group"][0].rearrange("(k p) n -> p k n", p=P)).then_inc(moe_in, 16)
                    sp.dma_start(wr[:, :, NGRP:NR], A["w_router_expert"][0].rearrange("(k p) n -> p k n", p=P)).then_inc(moe_in, 16)
                    sp.dma_start(r_bias[:, 0:NGRP], bcast(A["b_router_group"], NGRP)).then_inc(moe_in, 16)
                    sp.dma_start(r_bias[:, NGRP:NR], bcast(A["b_router_expert"], NE)).then_inc(moe_in, 16)
            src = {"gate": A["w_exp_gate"][0].rearrange("e (k p) n -> p e k n", p=P),
                   "up": A["w_exp_up"][0].rearrange("e (k p) n -> p e k n", p=P),
                   "down": A["w_exp_down"][0].rearrange("e (k p) n -> p e k n", p=P)}
            y_rows = y_d.rearrange("(s p) n -> p s n", p=P)

            def load(expert, e, r):
                for x in kinds:
                    if not (isinstance(e, int) and e < WRING):
                        sp.wait_ge(y_mm if x == "down" else gu_mm, e - WRING + 1 if r is not None else e)
                    slot = r or 0
                    sp.dma_start(m_raw[x][:, slot], src[x][:, bass.ds(expert, 1), :, :].rearrange("p e k n -> p (e k) n"))\
                      .then_inc(w_arrived[x][slot], 16)

            def store(e, p):
                sp.wait_ge(y_done, e + 1)
                sp.dma_start(y_rows[:, bass.ds(e, 1), :].rearrange("p s n -> p (s n)"), m_y[:, p, :]).then_inc(y_out[p], 16)

            need(sp, E_, mm, last_out + 1)
            for e in range(WRING):
                load(e, e, e)
                if e == 0:
                    sp.wait_ge(h2_out, 16 * NT)
            sp.wait_ge(mm, len(jobs.by))
            sp.wait_ge(over_done, 1)
            sp.dma_start(g_fin[:, :], bcast(A["norm_final"], D)).then_inc(gfin_in, 16)

            def tile(e, p, k, r, u):
                if ahead(e, WRING):
                    load(e + WRING, e + WRING, r)
                store(e, p)

            first_tiles(sp.Fori, tile)
            def beyond_tile(e, j, k, u):
                expert = sp.value_load(over_row[0:1, bass.ds(j, 1)], min_val=0, max_val=NE - 1)
                load(expert, e, None)
                store(e, 0)

            beyond(sp, beyond_tile)
            for i in range(NT):
                sp.wait_ge(fin_done, i + 1)
                out, r = (outs[0], i) if i < S_PROMPT // P else (outs[1], i - S_PROMPT // P)
                sp.dma_start(out[0, r * P:(r + 1) * P, :], y_fin[:, i, :]).then_inc(out_done, 16)
            sp.wait_ge(out_done, 16 * NT)

        @block.gpsimd
        def _(pool):
            E_ = "pool"

            def link(ins):
                counts["pool"] += 1
                ins.then_inc(pool_chain, 1)
                pool.wait_ge(pool_chain, counts["pool"])

            pool.memset(relx[NBK:NBK + 1, :], 1.0).then_inc(consts, 1)
            pool.wait_ge(consts, 1)
            link(pool.memset(eps[:, :], EPS))
            link(pool.memset(zeros[:, :], 0.0))
            link(pool.memset(ident[:, :], 0.0))
            link(pool.affine_select(out=ident[:, :], in_=ident[:, :], compare_op=ALU.not_equal, fill=1.0,
                                    base=0, pattern=[[-1, P]], channel_multiplier=1))
            link(pool.memset(mask_f[:, :], 1))
            link(pool.memset(mask_b[:, :], 1))
            link(pool.affine_select(out=mask_f[:, :], in_=mask_f[:, :], compare_op=ALU.is_ge, fill=0,
                                    base=0, pattern=[[1, P]], channel_multiplier=-1))
            link(pool.affine_select(out=mask_b[:, :], in_=mask_b[:, :], compare_op=ALU.is_ge, fill=0,
                                    base=-1, pattern=[[-1, P]], channel_multiplier=1))
            link(pool.memset(mask_f[0:CH, CH:P], 0))
            link(pool.memset(mask_b[CH:P, 0:CH], 0))
            link(pool.memset(scan_mask[:, :], 1.0))
            link(pool.memset(scan_mask[:, :].rearrange("p (c t) -> p c t", t=CH)[:, :, 0:1], 0.0))
            pool.memset(scan_mask[:, 0:1], 0.0).then_inc(consts, 1)
            pool.wait_ge(consts, 2)

            pads, gs, mls = [0], [0], [0]
            for s in steps:
                if s.kind == "w":
                    gs[0] = s.g + 1
                    g = s.g
                    if g == 2:
                        need(pool, E_, mm, last_hT + 1)
                        need(pool, E_, dve_evac, jobs.evac[last_hT])
                        need(pool, E_, wlo_done, g)
                        link(pool.memset(pad[:, :, 0:CH], 0.0))
                        pool.memset(pad[:, :, 3 * P - CH:3 * P], 0.0).then_inc(pad_zero, 1)
                        pads[0] = 1
                    if dve_splits(g):
                        continue
                    kb, n = group_shape(g)
                    need(pool, E_, whi_done, g + 1)
                    need(pool, E_, wlo_done, g)
                    need(pool, E_, mlo_done, mls[0])
                    need(pool, E_, pad_zero, pads[0])
                    pool.tensor_tensor(w_lo[:, g % 2, 0:kb, 0:n], raw[:, g % 2, 0:kb, 0:n],
                                       w_hi[:, g % 2, 0:kb, 0:n].bitcast(F32), ALU.subtract).then_inc(wlo_done, 1)
                elif s.kind == "comb" or (s.kind == "z" and s.h and s.d == 0 and s.s == 0):
                    h = s.h or 0
                    if h == 0:
                        need(pool, E_, mm, units[-1].sc + 1)
                        need(pool, E_, wlo_done, gs[0])
                        link(pool.memset(wgate[:, :, :], 0.0))
                        link(pool.memset(ptg[:, :, :], 0.0))
                    else:
                        need(pool, E_, mm, find(kind="z", h=h - 1)[-1].job + 1)
                    pool.dma_start(wgate[0:RANK, 0, :], A["w_gate_f"][0][:, h * DK:(h + 1) * DK]).then_inc(wg_in, 16)
                    pool.dma_start(wgate[RANK:2 * RANK, 1, :], A["w_gate_b"][0][:, h * DK:(h + 1) * DK]).then_inc(wg_in, 16)
                elif s.kind == "gstat":
                    need(pool, E_, mm, find(kind="o")[-1].job + 1)
                    pool.dma_start(g_gla[:, :], bcast(A["gla_norm"], DV)).then_inc(ggla_in, 16)
                elif s.kind == "mixT" and s.k < KD - 2:
                    need(pool, E_, wlo_done, gs[0])
                    need(pool, E_, mlo_done, s.k)
                    mls[0] = s.k + 1
                    need(pool, E_, mhi_done, s.k + 1)
                    pool.tensor_tensor(mT_lo[:, s.k, :], mixf[:, s.k, :], mT_hi[:, s.k, :].bitcast(F32),
                                       ALU.subtract).then_inc(mlo_done, 1)
                elif s.kind == "norm2" and s.i == 0:
                    need(pool, E_, wlo_done, gs[0])
                    need(pool, E_, mlo_done, KD)
                    link(pool.memset(m_x[:, :, :], 0.0))
                    link(pool.memset(ones[:, :], 1.0))
                    link(pool.memset(earlier[:, :], 1.0))
                    link(pool.affine_select(out=earlier[:, :], in_=earlier[:, :], compare_op=ALU.is_ge, fill=0.0,
                                            base=-1, pattern=[[1, P]], channel_multiplier=-1))
                    link(pool.iota(iota_row[:, :], pattern=[[1, P]], base=0, channel_multiplier=0,
                                   allow_small_or_imprecise_dtypes=True))
                    pool.iota(iota_tok[:, :], pattern=[[P, NT]], base=1, channel_multiplier=1,
                              allow_small_or_imprecise_dtypes=True).then_inc(rconst, 1)
                    pool.wait_ge(rconst, 1)
                elif s.kind == "h2T" and s.half == 0:
                    need(pool, E_, h2_done, s.i + 1)
                    pool.dma_start(h2_d[s.i * P:(s.i + 1) * P, :], h2[:, s.i, :]).then_inc(h2_out, 16)

            for e, x in ((0, "gate"), (0, "up"), (0, "down"), (1, "gate")):
                need(pool, E_, w_hi_done[x], e + 1)
                pool.tensor_tensor(m_lo[x][:, e], m_raw[x][:, e], m_hi[x][:, e].bitcast(F32),
                                   ALU.subtract).then_inc(w_lo_done[x], 1)
                need(pool, E_, w_lo_done[x], e + 1)
            evac_done(pool, E_, find(kind="table")[0].job)

            def take_idx(e, p, ring):
                if not (isinstance(e, int) and e < ring):
                    pool.wait_ge(xt_mm, e + (1 - ring))
                pool.tensor_copy(x_idx[:, p:p + 1], slot_idx[:, bass.ds(e, 1)]).then_inc(x_copied, 1)

            def lo_gate(e, p, r, copied):
                pool.wait_ge(w_hi_done["gate"], e + 1)
                pool.wait_ge(x_copied, copied)
                pool.tensor_tensor(m_lo["gate"][:, r], m_raw["gate"][:, r], m_hi["gate"][:, p].bitcast(F32),
                                   ALU.subtract).then_inc(w_lo_done["gate"], 1)

            def gather(p):
                pool.indirect_dma_start(m_x[:, p, :], None, h2_d,
                                        bass.IndirectOffsetOnAxis(ap=x_idx[:, p:p + 1].bitcast(U32), axis=0),
                                        bounds_check=T - 1, oob_is_err=False).then_inc(x_gathered[p], 16)

            pool.wait_ge(h2_out, 16 * NT)
            pool.wait_ge(zero_out, 16 * OVER)
            take_idx(0, 0, 2)
            pool.wait_ge(x_copied, 1)
            gather(0)
            take_idx(1, 1, 2)
            pool.wait_ge(x_copied, 2)
            gather(1)
            take_idx(2, 0, 2)
            pool.wait_ge(x_copied, 3)
            gather(0)

            def tile(e, p, k, r, u):
                if ahead(e, 3):
                    pool.wait_ge(w_lo_done["gate"], e + 2)
                    take_idx(e + 3, 1 - p, 2)
                if ahead(e, 2):
                    lo_gate(e + 2, p, later(r, u, 2)[0], e + 4 if ahead(e, 3) else NE)
                if ahead(e, 3):
                    gather(1 - p)

            first_tiles(pool.Fori, tile)

            def beyond_tile(e, j, k, u):
                pool.wait_ge(w_lo_done["gate"], e)
                take_idx(e, 0, 1)
                lo_gate(e, 0, 0, e + 1)
                gather(0)

            n_over = beyond(pool, beyond_tile)
            pool.wait_ge(y_out[0], (n_over + NE // 2) * 16)
            pool.wait_ge(y_out[1], NE // 2 * 16)
            pool.sem_inc(results_in, 1)
            pool.wait_ge(results_in, 1)
            pool.wait_ge(place_done, 1)
            for i in range(NT):
                for j in range(2):
                    pool.indirect_dma_start(y_pair[:, i, j, :], None, y_d,
                                            bass.IndirectOffsetOnAxis(ap=pair_idx[:, i, j:j + 1].bitcast(U32), axis=0),
                                            bounds_check=SLOTS * P - 1, oob_is_err=False).then_inc(pair_in[i], 16)

        @block.scalar
        def _(act):
            E_ = "act"

            def mark(ins):
                counts["act"] += 1
                ins.then_inc(act_chain, 1)

            def settle():
                need(act, E_, act_chain, counts["act"])

            def hi_weights(x, e, p, ring, r, u):
                act.wait_ge(w_arrived[x][r], u * 16 + 16)
                if not (isinstance(e, int) and e < ring):
                    act.wait_ge(y_mm if x == "down" else gu_mm, e + (1 - ring))
                act.activation(m_hi[x][:, p], m_raw[x][:, r], ACT.Copy).then_inc(w_hi_done[x], 1)

            for s in steps:
                k = s.kind
                if k == "w":
                    g = s.g
                    kb, n = group_shape(g)
                    need(act, E_, raw_in[g % 2], raw_value[g])
                    if g >= 2:
                        need(act, E_, mm, last_of_group[g - 2] + 1)
                    act.activation(w_hi[:, g % 2, 0:kb, 0:n], raw[:, g % 2, 0:kb, 0:n], ACT.Copy).then_inc(whi_done, 1)
                elif k == "vec":
                    need(act, E_, mm, s.job + 1)
                    act.activation(vecs[:, s.a, :], bank(s.job)[0:AH, 0:VEC], ACT.Copy)\
                       .then_inc(act_evac, 1)
                elif k == "norm":
                    i = s.i
                    need(act, E_, sq_done, i)
                    need(act, E_, x_in[i], 16)
                    act.activation(junk[:, :], xin[:, i, :], ACT.Square, accum_out=ss[:, i:i + 1]).then_inc(sq_done, 1)
                    need(act, E_, var_done, i + 1)
                    act.activation(std[:, i:i + 1], rstd[:, i:i + 1], ACT.Sqrt).then_inc(std_done, 1)
                elif k in ("hT", "oaT", "obT"):
                    need(act, E_, mm, s.job + 1)
                    if k == "hT":
                        out, src = hT_hi[:, 4 * s.half:4 * s.half + 4, s.i * P:(s.i + 1) * P], bank(s.job)[:, :]
                    elif k == "oaT":
                        out, src = oaT_hi[:, :, s.i * P:(s.i + 1) * P], bank(s.job)[:, 0:2 * P]
                    else:
                        out, src = obT_hi[:, 2 * s.h:2 * s.h + 2, s.i * P:(s.i + 1) * P], bank(s.job)[:, 0:2 * P]
                    act.activation(out, src.rearrange("p (k t) -> p k t", t=P), ACT.Copy).then_inc(hi_done, 1)
                elif k in ("ws", "ts") and jobs.by[s.job] == "act":
                    name, a = s.dest
                    need(act, E_, mm, s.job + 1)
                    b_ = bank(s.job)
                    if k == "ws":
                        src, tok = b_[:, 0:HALF], slice(s.s * HALF, (s.s + 1) * HALF)
                        if name in ("q", "k"):
                            x = qk[:, a % 2, s.b + (2 if name == "k" else 0), :]
                            for out, part in (by_class(x, src, s.s) if a else [(x[:, tok], src)]):
                                ins = act.activation(out, part, ACT.Copy, scale=HD ** -0.5 if name == "q" else 1.0)
                            ins.then_inc(act_evac, 1)
                        elif name == "gate":
                            act.activation(gT[:, tok], b_[0:2 * RANK, 0:HALF], ACT.Copy).then_inc(act_evac, 1)
                        elif name == "qkb":
                            if a >= 2:
                                need(act, E_, ko, 2 * (a - 2) + 2)
                            act.activation(qkb[a % 2][:, s.b, tok], src, ACT.Copy).then_inc(act_evac, 1)
                        else:
                            if a:
                                need(act, E_, dve_evac, jobs.evac[last_of_group[gnum["pb", a - 1]]])
                            act.activation((sga if name == "ma" else sgb)[:, s.b, tok], src, ACT.Sigmoid)\
                               .then_inc(act_evac, 1)
                    else:
                        src = b_[:, 0:GW]
                        if name == "v":
                            act.activation(va[:, a % 2, s.i, :], src, ACT.Copy).then_inc(act_evac, 1)
                        elif name == "vb":
                            act.activation(vb[:, s.i, :], src, ACT.Copy).then_inc(act_evac, 1)
                        else:
                            n = NT * a + s.i
                            if n >= 2:
                                need(act, E_, ob_done, n - 1)
                            act.activation(sg[:, n % 2, :], src, ACT.Silu).then_inc(act_evac, 1)
                elif k == "sc":
                    u = s.u
                    need(act, E_, neg_max, u.n + 1)
                    for hh, h in enumerate(u.heads):
                        if u.a == 0:
                            if u.n >= 2:
                                need(act, E_, mm, units[u.n - 2].pt + 1)
                            out = pad[:, u.n % 2, CH + u.lo:CH + u.lo + u.width]
                        else:
                            out = sc[:, u.n % 3, hh * u.width:(hh + 1) * u.width]
                        ins = act.activation(out, sc[:, u.n % 3, hh * u.width:(hh + 1) * u.width], ACT.Exp,
                                             bias=nmx[:, u.i, u.a, h:h + 1],
                                             accum_out=o_att[:, u.i, u.a, AW + AH + h:AW + AH + h + 1])
                    ins.then_inc(probs, 1)
                elif k == "pt" and jobs.by[s.job] == "act":
                    u = s.u
                    n = len(u.heads) * len(u.ktiles) * P
                    need(act, E_, mm, s.job + 1)
                    act.activation(ptr[:, u.n % 3, 0:n], bank(s.job)[:, 0:n], ACT.Copy).then_inc(act_evac, 1)
                elif k == "pv":
                    u = s.u
                    nh, hs = len(u.heads), slice(u.heads[0], u.heads[-1] + 1, 2)
                    need(act, E_, mm, s.job + 1)
                    act.activation(o_att[:, u.i, u.a, 0:AW].rearrange("p (h d) -> p h d", d=HD)[:, hs, :],
                                   bank(s.job)[:, 0:nh * HD].rearrange("p (h d) -> p h d", d=HD), ACT.Copy)\
                       .then_inc(act_evac, 1)
                elif k == "comb":
                    need(act, E_, comb_neg, 1)
                    act.activation(nmx[:, :, :, :], o_att[:, :, :, MAX], ACT.Exp).then_inc(comb_exp, 1)
                elif k == "z":
                    need(act, E_, mm, s.job + 1)
                    need(act, E_, bias_in, 32)
                    if s.h:
                        need(act, E_, ko, 2 * s.h)
                    act.activation(zt[:, s.d, s.s * HALF:(s.s + 1) * HALF], bank(s.job)[:, 0:HALF], ACT.Identity,
                                   bias=gate_bias[:, s.d, s.h:s.h + 1]).then_inc(act_evac, 1)
                elif k == "decay":
                    h = s.h
                    if h:
                        need(act, E_, mm, find(kind="kot", h=h - 1)[-1].job + 1)
                    for d in range(2):
                        need(act, E_, act_evac, jobs.evac[find(kind="z", h=h, d=d, s=1)[0].job])
                        mark(act.activation(et[:, d, :], zt[:, d, :], ACT.Abs))
                    settle()
                    for d in range(2):
                        mark(act.activation(et[:, d, :], et[:, d, :], ACT.Exp, scale=-1.0))
                    settle()
                    for d in range(2):
                        act.activation(et[:, d, :], et[:, d, :], ACT.Ln, bias=1.0).then_inc(softplus, 1)
                    for d in range(2):
                        need(act, E_, cum, 2 * h + d + 1)
                        last = zt[:, d, :].rearrange("p (c t) -> p c t", t=CH)[:, :, (CH - 1 if d == 0 else 0)]
                        act.activation(et[:, d, :], zt[:, d, :], ACT.Exp, scale=1.0 / 16).then_inc(e1, 1)
                        act.activation(dec[:, h % 2, d, :], last, ACT.Exp, scale=1.0 / 16).then_inc(e1, 1)
                    for d in range(2):
                        need(act, E_, qin, 2 * h + d + 1)
                        act.activation(et[:, d, :], zt[:, d, :], ACT.Exp, scale=-1.0 / 16).then_inc(e2, 1)
                    for d in range(2):
                        need(act, E_, dd, 2 * h + d + 1)
                        act.activation(et[:, d, :], et[:, d, :], ACT.Exp, scale=1.0 / 16).then_inc(e3, 1)
                elif k == "kot":
                    need(act, E_, mm, s.job + 1)
                    act.activation(kot[:, 4 * s.q:4 * s.q + 4, :].rearrange("p a b -> p (a b)"), bank(s.job)[:, :],
                                   ACT.Copy).then_inc(act_evac, 1)
                elif k == "o":
                    need(act, E_, dve_evac, jobs.evac[s.job])
                    need(act, E_, gla_sq, s.seq)
                    act.activation(junk_gla[:, :], o_gla[:, s.i, s.h * DV:(s.h + 1) * DV], ACT.Square,
                                   accum_out=gss[:, s.i, s.h:s.h + 1]).then_inc(gla_sq, 1)
                elif k == "gstat":
                    need(act, E_, gvar, 1)
                    act.activation(gstd[:, :, :], grstd[:, :, :], ACT.Sqrt).then_inc(gstd_done, 1)
                elif k == "mixT":
                    need(act, E_, mm, last_of_group[gnum["mb", 3]] + 1)
                    need(act, E_, dve_evac, jobs.evac[last_of_group[gnum["pb", s.k // 2]]])
                    act.activation(mT_hi[:, s.k, :], mixf[:, s.k, :], ACT.Copy).then_inc(mhi_done, 1)
                elif k == "norm2":
                    i = s.i
                    need(act, E_, dve_evac, jobs.evac[find(kind="ts", dest=("out", 3), i=i)[0].job])
                    need(act, E_, sq2, i)
                    act.activation(junk2[:, :], x1[:, i, :], ACT.Square, accum_out=ss[:, i:i + 1]).then_inc(sq2, 1)
                    need(act, E_, var2, i + 1)
                    act.activation(std[:, i:i + 1], rstd[:, i:i + 1], ACT.Sqrt).then_inc(std2, 1)
                elif k == "h2T":
                    need(act, E_, mm, s.job + 1)
                    act.activation(h2T[:, s.i % 2, 4 * s.half:4 * s.half + 4, :],
                                   bank(s.job)[:, :].rearrange("p (k t) -> p k t", t=P), ACT.Copy).then_inc(act_evac, 1)
                elif k == "route":
                    need(act, E_, mm, last_out + 1)
                    need(act, E_, mlo_done, KD)
                    hi_weights("gate", 0, 0, 2, 0, 0)
                    hi_weights("up", 0, 0, 2, 0, 0)
                    need(act, E_, route_neg, 1)
                    act.activation(ex[:, :, :], ex[:, :, :], ACT.Exp).then_inc(route_exp, 1)
                    hi_weights("down", 0, 0, 2, 0, 0)
                    need(act, E_, route_neg2, 1)
                    act.activation(ratio[:, :], ratio[:, :], ACT.Exp).then_inc(route_exp2, 1)
                    for x in kinds:
                        hi_weights(x, 1, 1, 2, 1, 0)

            def hi_x(e, p, ring):
                act.wait_ge(xt_mm, e + 1)
                if not (isinstance(e, int) and e < ring):
                    act.wait_ge(gu_mm, e + (1 - ring))
                for half in range(2):
                    ins = act.activation(m_xT_hi[:, p, 4 * half:4 * half + 4, :],
                                         psum[B_XT[half]][:, :].rearrange("p (k t) -> p k t", t=P), ACT.Copy)
                ins.then_inc(xt_hi, 1)

            def silu(e, p, ring):
                act.wait_ge(gu_mm, e + 1)
                if not (isinstance(e, int) and e < ring):
                    act.wait_ge(a_done, e + (1 - ring))
                act.activation(m_sil[:, p, :], psum[B_GU[p]][:, 0:FF], ACT.Silu).then_inc(silu_done, 1)

            def hi_a(e, p, ring):
                act.wait_ge(at_mm, e + 1)
                if not (isinstance(e, int) and e < ring):
                    act.wait_ge(y_mm, e + (1 - ring))
                act.activation(m_aT_hi[:, p, :, :], psum[B_AT[p]][:, 0:2 * P].rearrange("p (k t) -> p k t", t=P), ACT.Copy)\
                   .then_inc(at_hi, 1)

            hi_x(0, 0, 2)
            hi_x(1, 1, 2)

            def tile(e, p, k, r, u):
                silu(e, p, 2)
                if ahead(e, 2):
                    hi_weights("gate", e + 2, p, 2, *later(r, u, 2))
                    hi_weights("up", e + 2, p, 2, *later(r, u, 2))
                hi_a(e, p, 2)
                if ahead(e, 2):
                    hi_x(e + 2, p, 2)
                if ahead(e, 1) and not first(e):
                    hi_weights("down", e + 1, 1 - p, 2, *later(r, u, 1))

            first_tiles(act.Fori, tile)

            def beyond_tile(e, j, k, u):
                for x in kinds:
                    hi_weights(x, e, 0, 1, 0, u)
                hi_x(e, 0, 1)
                silu(e, 0, 1)
                hi_a(e, 0, 1)

            beyond(act, beyond_tile)
            for i in range(NT):
                act.wait_ge(sum_done, i + 1)
                act.activation(junk3[:, :], x1[:, i, :], ACT.Square, accum_out=ss[:, i:i + 1]).then_inc(sq3, 1)
                act.wait_ge(sq3, i + 1)
                act.activation(std[:, i:i + 1], ss[:, i:i + 1], ACT.Sqrt, scale=1.0 / D, bias=eps[:, 0:1]).then_inc(std3, 1)

        @block.tensor
        def _(pe):
            E_ = "pe"

            def claim(s):
                if s.job >= BANKS:
                    evac_done(pe, E_, s.job - BANKS)

            def product3(out, pairs, split=None):
                n = len(pairs)
                for j, (l_hi, l_lo, r_hi, r_lo) in enumerate(pairs):
                    if split is not None:
                        need(pe, E_, split, j + 1)
                    pe.matmul(out, l_hi, r_hi, start=j == 0, stop=False)
                    pe.matmul(out, l_hi, r_lo, start=False, stop=False)
                    ins = pe.matmul(out, l_lo, r_hi, start=False, stop=j == n - 1)
                return ins

            for s in steps:
                k = s.kind
                if k in ("w", "norm", "natural", "comb", "mix", "decay", "gstat", "mixT", "norm2", "route", "place"):
                    continue
                claim(s)
                b_ = bank(s.job)
                if k == "vec":
                    need(pe, E_, rel_in, 32)
                    need(pe, E_, consts, 1)
                    ins = pe.matmul(b_[0:AH, 0:VEC], relx[:, (s.a + 1) // 2 * AH:((s.a + 1) // 2 + 1) * AH], onehot[:, s.a, :],
                                    start=True, stop=True)
                elif k == "hT":
                    need(pe, E_, consts, 2)
                    need(pe, E_, xn_done, s.i + 1)
                    for c in range(4):
                        ins = pe.transpose(b_[:, c * P:(c + 1) * P],
                                           xin[:, s.i, (4 * s.half + c) * P:(4 * s.half + c + 1) * P], ident[:, :])
                elif k in ("ws", "ts"):
                    g, (name, a) = s.g, s.dest
                    kb, n = group_shape(g)
                    need(pe, E_, wlo_done, g + 1)
                    x_hi, x_lo = {"pa": (oaT_hi, oaT_lo), "pb": (obT_hi, obT_lo), "out": (mT_hi, mT_lo)}\
                        .get(name, (hT_hi, hT_lo))
                    if name == "pa":
                        evac_done(pe, E_, find(kind="oaT")[-1].job)
                    elif name == "pb":
                        evac_done(pe, E_, find(kind="obT")[-1].job)
                    elif name != "out":
                        evac_done(pe, E_, last_hT)
                    if k == "ws":
                        m = min(P, n)
                        tok = slice(s.s * HALF, (s.s + 1) * HALF)
                        ins = product3(b_[0:m, 0:HALF],
                                       [(w_hi[:, g % 2, j, s.b * P:s.b * P + m], w_lo[:, g % 2, j, s.b * P:s.b * P + m],
                                         x_hi[:, j, tok], x_lo[:, j, tok]) for j in range(kb)])
                    else:
                        def tokens(x):
                            if name != "v" or s.dest[1] == 0:
                                return x[:, s.i * P:(s.i + 1) * P]
                            first, n = SEQS[0] if s.i < SEQS[1][0] else SEQS[1]
                            return x[:, first * P:(first + n) * P].rearrange("p (u r) -> p r u", r=n)[:, s.i - first, :]

                        ins = product3(b_[:, 0:GW],
                                       [(tokens(x_hi[:, j, :]), tokens(x_lo[:, j, :]), w_hi[:, g % 2, j, :], w_lo[:, g % 2, j, :])
                                        for j in range(kb)], split=mlo_done if name == "out" else None)
                elif k == "sc":
                    u = s.u
                    evac_done(pe, E_, last_of_group[gnum["k", u.a]])
                    k0 = P * (u.i - 1) + CH + u.lo if u.a == 0 else u.first * P
                    for hh, h in enumerate(u.heads):
                        rows = slice(HD * (h % 2), HD * (h % 2) + HD)
                        ins = pe.matmul(b_[:, hh * u.width:(hh + 1) * u.width],
                                        qk[rows, u.a % 2, h // 2, u.i * P:(u.i + 1) * P],
                                        qk[rows, u.a % 2, 2 + h // 2, k0:k0 + u.width], start=True, stop=True)
                elif k == "pt":
                    u = s.u
                    need(pe, E_, probs, u.n + 1)
                    if u.a == 0:
                        need(pe, E_, pad_zero, 1)
                        src = [pad[:, u.n % 2, (t - u.i + 1) * P:(t - u.i + 2) * P] for t in u.ktiles]
                    else:
                        src = [sc[:, u.n % 3, (hh * len(u.ktiles) + j) * P:(hh * len(u.ktiles) + j + 1) * P]
                               for hh in range(len(u.heads)) for j in range(len(u.ktiles))]
                    for j, x in enumerate(src):
                        ins = pe.transpose(b_[:, j * P:(j + 1) * P], x, ident[:, :])
                elif k == "pv":
                    u = s.u
                    evac_done(pe, E_, u.pt)
                    evac_done(pe, E_, last_of_group[gnum["v", u.a]])
                    nk = len(u.ktiles)
                    for hh, h in enumerate(u.heads):
                        for j, t in enumerate(u.ktiles):
                            x = (hh * nk + j) * P
                            ins = pe.matmul(b_[:, hh * HD:(hh + 1) * HD], ptr[:, u.n % 3, x:x + P],
                                            va[:, u.a % 2, t, h * HD:(h + 1) * HD], start=j == 0, stop=j == nk - 1)
                elif k == "oaT":
                    need(pe, E_, oa_done, s.i + 1)
                    for c in range(2):
                        ins = pe.transpose(b_[:, c * P:(c + 1) * P], o_att[:, s.i, 0, c * P:(c + 1) * P], ident[:, :])
                elif k == "z":
                    need(pe, E_, wg_in, 32 * (s.h + 1))
                    evac_done(pe, E_, last_of_group[gnum["gate", 0]])
                    ins = pe.matmul(b_[:, 0:HALF], wgate[:, s.d, :], gT[:, s.s * HALF:(s.s + 1) * HALF],
                                    start=True, stop=True)
                elif k == "kot":
                    for j in range(4):
                        d, t = divmod(4 * s.q + j, NT)
                        need(pe, E_, ko, 2 * s.h + d + 1)
                        ins = pe.transpose(b_[:, j * P:(j + 1) * P], et[:, d, t * P:(t + 1) * P], ident[:, :])
                elif k == "state":
                    evac_done(pe, E_, find(kind="kot", h=s.h)[-1].job)
                    evac_done(pe, E_, last_of_group[gnum["vb", s.h]])
                    c = 2 * s.first + (s.t if s.d == 0 else s.nc - 1 - s.t)
                    rows = slice(CH * (c % 2), CH * (c % 2) + CH)
                    ins = pe.matmul(b_[:, 0:DV], kot[rows, s.d * NT + c // 2, :], vb[rows, c // 2, :],
                                    start=True, stop=True)
                elif k == "intra":
                    need(pe, E_, kin, 2 * s.h + 2)
                    tok = slice(s.i * P, (s.i + 1) * P)
                    for d in range(2):
                        ins = pe.matmul(b_[:, d * P:(d + 1) * P], k_in[:, d, tok], q_in[:, d, tok], start=True, stop=True)
                elif k == "o":
                    it = find(kind="intra", h=s.h, i=s.i)[0]
                    evac_done(pe, E_, it.job)
                    stt = find(kind="state", h=s.h, first=s.first)
                    evac_done(pe, E_, stt[-1].job)
                    nch = 2 * s.n
                    parts = []
                    for half in range(2):
                        c = 2 * (s.i - s.first) + half
                        tok = slice(s.i * P + half * CH, s.i * P + (half + 1) * CH)
                        if c > 0:
                            parts.append((half, q_in[:, 0, tok], st[:, 0, c - 1, :]))
                        if c < nch - 1:
                            parts.append((half, q_in[:, 1, tok], st[:, 1, nch - 2 - c, :]))
                    pe.matmul(b_[:, 0:DV], ptg[:, it.seq % 2, :], vb[:, s.i, :], start=True, stop=False,
                              skip_group_check=True)
                    for j, (half, l, r) in enumerate(parts):
                        ins = pe.matmul(b_[half * CH:(half + 1) * CH, 0:DV], l, r, start=False,
                                        stop=j == len(parts) - 1, skip_group_check=True)
                elif k == "obT":
                    need(pe, E_, ob_done, NT * s.h + s.i + 1)
                    for c in range(2):
                        x = s.h * DV + c * P
                        ins = pe.transpose(b_[:, c * P:(c + 1) * P], o_gla[:, s.i, x:x + P], ident[:, :])
                elif k == "h2T":
                    need(pe, E_, h2_done, s.i + 1)
                    for c in range(4):
                        ins = pe.transpose(b_[:, c * P:(c + 1) * P],
                                           h2[:, s.i, (4 * s.half + c) * P:(4 * s.half + c + 1) * P], ident[:, :])
                elif k == "router":
                    need(pe, E_, moe_in, 5 * 16)
                    evac_done(pe, E_, find(kind="h2T", i=s.i)[-1].job)
                    for j in range(KD):
                        ins = pe.matmul(b_[:, 0:NR], h2T[:, s.i % 2, j, :], wr[:, j, :], start=j == 0, stop=j == KD - 1)
                elif k == "rank":
                    need(pe, E_, hot_done, 1)
                    pe.matmul(b_[:, 0:NT * NE], ones[:, :], before[:, 0:NT, :], start=True, stop=False)
                    pe.matmul(b_[:, 0:NT * NE], earlier[:, :], both[:, :, :], start=False, stop=True)
                    ins = pe.matmul(b_[:, NT * NE:(NT + 1) * NE], ones[:, :], before[:, NT, :], start=True, stop=True)
                elif k == "table":
                    need(pe, E_, place_done, 1)
                    for j in range(2 * NT):
                        ins = pe.matmul(b_[:, 0:EVEN], row_hot[:, j, :], slot_hot[:, j, :], start=j == 0, stop=j == 2 * NT - 1)
                ins.then_inc(mm, 1)

            def xt(e, p, k):
                pe.wait_ge(x_gathered[p], k * 16 + 16)
                if not (isinstance(e, int) and e == 0):
                    pe.wait_ge(xt_lo, e)
                for c in range(KD):
                    ins = pe.transpose(psum[B_XT[c // 4]][:, (c % 4) * P:(c % 4 + 1) * P], m_x[:, p, c * P:(c + 1) * P],
                                       ident[:, :])
                ins.then_inc(xt_mm, 1)

            def gate_up(e, p, r, ring):
                pe.wait_ge(xt_lo, e + 1)
                if not (isinstance(e, int) and e < ring):
                    pe.wait_ge(a_done, e + (1 - ring))
                for n, x in enumerate(("gate", "up")):
                    pe.wait_ge(w_lo_done[x], e + 1)
                    ins = product3(psum[B_GU[p]][:, n * FF:(n + 1) * FF],
                                   [(m_xT_hi[:, p, j, :], m_xT_lo[:, p, j, :], m_hi[x][:, p, j, :], m_lo[x][:, r, j, :])
                                    for j in range(KD)])
                ins.then_inc(gu_mm, 1)

            def aT(e, p, ring):
                pe.wait_ge(a_done, e + 1)
                if not (isinstance(e, int) and e < ring):
                    pe.wait_ge(at_lo, e + (1 - ring))
                for c in range(2):
                    ins = pe.transpose(psum[B_AT[p]][:, c * P:(c + 1) * P], m_a[:, p, c * P:(c + 1) * P], ident[:, :])
                ins.then_inc(at_mm, 1)

            def down(e, p, r):
                pe.wait_ge(at_lo, e + 1)
                pe.wait_ge(w_lo_done["down"], e + 1)
                if not (isinstance(e, int) and e == 0):
                    pe.wait_ge(y_done, e)
                for half in range(2):
                    cols = slice(half * 512, (half + 1) * 512)
                    ins = product3(psum[B_Y[half]][:, :],
                                   [(m_aT_hi[:, p, j, :], m_aT_lo[:, p, j, :], m_hi["down"][:, p, j, cols],
                                     m_lo["down"][:, r, j, cols]) for j in range(2)])
                ins.then_inc(y_mm, 1)

            need(pe, E_, dve_evac, jobs.count["dve"])
            need(pe, E_, act_evac, jobs.count["act"])
            xt(0, 0, 0)
            xt(1, 1, 0)
            gate_up(0, 0, 0, 2)

            def tile(e, p, k, r, u):
                if ahead(e, 1):
                    gate_up(e + 1, 1 - p, later(r, u, 1)[0], 2)
                aT(e, p, 2)
                if ahead(e, 2):
                    xt(e + 2, p, k + 1)
                down(e, p, r)

            first_tiles(pe.Fori, tile)

            def beyond_tile(e, j, k, u):
                xt(e, 0, k)
                gate_up(e, 0, 0, 1)
                aT(e, 0, 1)
                down(e, 0, 0)

            beyond(pe, beyond_tile)

        @block.vector
        def _(dve):
            E_ = "dve"

            def mark(ins):
                counts["dve"] += 1
                ins.then_inc(dve_chain, 1)

            def settle():
                need(dve, E_, dve_chain, counts["dve"])

            def link(ins):
                mark(ins)
                settle()

            wide = lambda x, n: x.rearrange("p (i o) -> p i o", o=1).broadcast_to([P, NT, n])
            for s in steps:
                k = s.kind
                if k == "ts" and s.dest[0] == "og":
                    h, i = s.dest[1], s.i
                    x = o_gla[:, i, h * DV:(h + 1) * DV]
                    link(dve.scalar_tensor_tensor(x, x, grstd[:, i, h:h + 1], g_gla[:, :], ALU.mult, ALU.mult))
                    evac_done(dve, E_, s.job)
                    dve.tensor_tensor(x, x, sg[:, (NT * h + i) % 2, :], ALU.mult).then_inc(ob_done, 1)
                    continue
                if s.job is not None:
                    if jobs.by[s.job] != "dve":
                        continue
                    b_ = bank(s.job)
                if k == "w" and dve_splits(s.g):
                    g = s.g
                    kb, n = group_shape(g)
                    need(dve, E_, whi_done, g + 1)
                    if g:
                        need(dve, E_, wlo_done, g)
                    dve.tensor_tensor(w_lo[:, g % 2, 0:kb, 0:n], raw[:, g % 2, 0:kb, 0:n],
                                      w_hi[:, g % 2, 0:kb, 0:n].bitcast(F32), ALU.subtract).then_inc(wlo_done, 1)
                elif k == "mixT" and s.k >= KD - 2:
                    need(dve, E_, mhi_done, s.k + 1)
                    need(dve, E_, mlo_done, s.k)
                    dve.tensor_tensor(mT_lo[:, s.k, :], mixf[:, s.k, :], mT_hi[:, s.k, :].bitcast(F32),
                                      ALU.subtract).then_inc(mlo_done, 1)
                elif k == "norm":
                    i = s.i
                    need(dve, E_, sq_done, i + 1)
                    dve.tensor_scalar(rstd[:, i:i + 1], ss[:, i:i + 1], 1.0 / D, EPS, ALU.mult, ALU.add).then_inc(var_done, 1)
                    need(dve, E_, std_done, i + 1)
                    link(dve.reciprocal(rstd[:, i:i + 1], std[:, i:i + 1]))
                    need(dve, E_, gmix_in, 16)
                    dve.scalar_tensor_tensor(xin[:, i, :], xin[:, i, :], rstd[:, i:i + 1], g_mix[:, :],
                                             ALU.mult, ALU.mult).then_inc(xn_done, 1)
                elif k in ("hT", "oaT", "obT"):
                    need(dve, E_, hi_done, s.hi)
                    if k == "hT":
                        ks, lo, hi = slice(4 * s.half, 4 * s.half + 4), hT_lo, hT_hi
                    elif k == "oaT":
                        ks, lo, hi = slice(0, 2), oaT_lo, oaT_hi
                    else:
                        ks, lo, hi = slice(2 * s.h, 2 * s.h + 2), obT_lo, obT_hi
                    tok, n = slice(s.i * P, (s.i + 1) * P), (ks.stop - ks.start) * P
                    dve.tensor_tensor(lo[:, ks, tok], b_[:, 0:n].rearrange("p (k t) -> p k t", t=P),
                                      hi[:, ks, tok].bitcast(F32), ALU.subtract).then_inc(dve_evac, 1)
                elif k in ("ws", "ts"):
                    name, a = s.dest
                    need(dve, E_, mm, s.job + 1)
                    if name == "pa":
                        tok = slice(s.s * HALF, (s.s + 1) * HALF)
                        evac_done(dve, E_, last_of_group[gnum["ma", a]])
                        dve.tensor_tensor(sga[:, s.b, tok], sga[:, s.b, tok], b_[:, 0:HALF], ALU.mult).then_inc(dve_evac, 1)
                    elif name == "pb":
                        tok = slice(s.s * HALF, (s.s + 1) * HALF)
                        evac_done(dve, E_, last_of_group[gnum["mb", a]])
                        evac_done(dve, E_, last_of_group[gnum["pa", a]])
                        link(dve.tensor_tensor(sgb[:, s.b, tok], sgb[:, s.b, tok], b_[:, 0:HALF], ALU.mult))
                        dve.tensor_tensor(mixf[:, 2 * a + s.b, tok], sga[:, s.b, tok], sgb[:, s.b, tok],
                                          ALU.add).then_inc(dve_evac, 1)
                    else:
                        cols = slice(a * GW, (a + 1) * GW)
                        need(dve, E_, x1_in[s.i], 16)
                        dve.tensor_tensor(x1[:, s.i, cols], x1[:, s.i, cols], b_[:, 0:GW], ALU.add).then_inc(dve_evac, 1)
                elif k == "sc":
                    u = s.u
                    need(dve, E_, mm, s.job + 1)
                    need(dve, E_, table_in, 16 * NV)
                    if u.n >= 3:
                        need(dve, E_, mm, units[u.n - 3].pt + 1)
                    for hh, h in enumerate(u.heads):
                        cols = slice(hh * u.width, (hh + 1) * u.width)
                        bias = (table[0][:, h, u.lo:u.lo + u.width] if u.a == 0 else
                                table[u.a][:, 0 if u.i < SEQS[1][0] else 1, h, :])
                        ins = dve.tensor_tensor_reduce(out=sc[:, u.n % 3, cols], in0=b_[:, cols],
                                                       in1=bias, scale=1.0, scalar=-3e38, op0=ALU.add, op1=ALU.max,
                                                       accum_out=o_att[:, u.i, u.a, AW + h:AW + h + 1])
                    ins.then_inc(dve_evac, 1)
                    need(dve, E_, dve_evac, jobs.evac[s.job])
                    hs = slice(u.heads[0], u.heads[-1] + 1, 2)
                    dve.tensor_scalar(nmx[:, u.i, u.a, hs], o_att[:, u.i, u.a, MAX][:, hs], -1.0, None,
                                      ALU.mult).then_inc(neg_max, 1)
                elif k == "pt":
                    u = s.u
                    n = len(u.heads) * len(u.ktiles) * P
                    need(dve, E_, mm, s.job + 1)
                    dve.tensor_copy(ptr[:, u.n % 3, 0:n], b_[:, 0:n]).then_inc(dve_evac, 1)
                elif k == "comb":
                    for x in att_in:
                        need(dve, E_, x, 16)
                    settle()
                    mx, sm = o_att[:, :, :, MAX], o_att[:, :, :, SUM]
                    link(dve.tensor_tensor(cm[:, :, :], mx[:, :, 0, :], mx[:, :, 1, :], ALU.max))
                    link(dve.tensor_tensor(cm[:, :, :], cm[:, :, :], mx[:, :, 2, :], ALU.max))
                    for a in range(NG):
                        ins = dve.tensor_tensor(mx[:, :, a, :], mx[:, :, a, :], cm[:, :, :], ALU.subtract)
                        if a < NG - 1:
                            mark(ins)
                    ins.then_inc(comb_neg, 1)
                    need(dve, E_, comb_exp, 1)
                    link(dve.tensor_tensor(wgrp[:, :, :, :], nmx[:, :, :, :], sm, ALU.mult))
                    link(dve.tensor_tensor(cden[:, :, :], wgrp[:, :, 0, :], wgrp[:, :, 1, :], ALU.add))
                    link(dve.tensor_tensor(cden[:, :, :], cden[:, :, :], wgrp[:, :, 2, :], ALU.add))
                    link(dve.reciprocal(cden[:, :, :], cden[:, :, :]))
                    for a in range(NG):
                        mark(dve.tensor_tensor(wgrp[:, :, a, :], nmx[:, :, a, :], cden[:, :, :], ALU.mult))
                elif k == "mix":
                    i = s.i
                    settle()
                    for a in range(NG):
                        x = o_att[:, i, a, 0:AW].rearrange("p (h d) -> p h d", d=HD)
                        wv = wgrp[:, i, a, :].rearrange("p (h o) -> p h o", o=1).broadcast_to([P, AH, HD])
                        mark(dve.tensor_tensor(x, x, wv, ALU.mult))
                    settle()
                    o0, o1, o2 = (o_att[:, i, a, 0:AW] for a in range(NG))
                    link(dve.tensor_tensor(o0, o0, o1, ALU.add))
                    dve.tensor_tensor(o0, o0, o2, ALU.add).then_inc(oa_done, 1)
                elif k == "decay":
                    h = s.h
                    q, kk = qkb[h % 2][:, 0, :], qkb[h % 2][:, 1, :]
                    chunks = lambda x: x.rearrange("p (c t) -> p c t", t=CH)
                    for d in range(2):
                        need(dve, E_, softplus, 2 * h + d + 1)
                        mark(dve.scalar_tensor_tensor(zt[:, d, :], zt[:, d, :], 0.0, et[:, d, :], ALU.min, ALU.subtract))
                    settle()
                    for d in range(2):
                        x = zt[:, d, :] if d == 0 else zt[:, d, ::-1]
                        dve.tensor_tensor_scan(x, scan_mask[:, :], x, 0.0, ALU.mult, ALU.add).then_inc(cum, 1)
                    for d in range(2):
                        need(dve, E_, e1, 4 * h + 2 * d + 2)
                        evac_done(dve, E_, last_of_group[gnum["qkb", h]])
                        if h:
                            need(dve, E_, mm, find(kind="o", h=h - 1)[-1].job + 1)
                        dve.scalar_tensor_tensor(q_in[:, d, :], q, DK ** -0.5, et[:, d, :], ALU.mult, ALU.mult).then_inc(qin, 1)
                    for d in range(2):
                        need(dve, E_, e2, 2 * h + d + 1)
                        dve.tensor_tensor(k_in[:, d, :], kk, et[:, d, :], ALU.mult).then_inc(kin, 1)
                        need(dve, E_, kin, 2 * h + d + 1)
                        b = chunks(zt[:, d, :])
                        at_ = CH - 1 if d == 0 else 0
                        dve.tensor_tensor(chunks(et[:, d, :]), b[:, :, at_:at_ + 1].broadcast_to([P, NCH, CH]), b,
                                          ALU.subtract).then_inc(dd, 1)
                    for d in range(2):
                        need(dve, E_, e3, 2 * h + d + 1)
                        dve.tensor_tensor(et[:, d, :], kk, et[:, d, :], ALU.mult).then_inc(ko, 1)
                elif k == "state":
                    need(dve, E_, mm, s.job + 1)
                    c = 2 * s.first + (s.t if s.d == 0 else s.nc - 1 - s.t)
                    if s.t == 0:
                        dve.tensor_copy(st[:, s.d, 0, :], b_[:, 0:DV]).then_inc(dve_evac, 1)
                    else:
                        need(dve, E_, dve_evac, jobs.evac[s.prev])
                        dve.scalar_tensor_tensor(st[:, s.d, s.t, :], st[:, s.d, s.t - 1, :], dec[:, s.h % 2, s.d, c:c + 1],
                                                 b_[:, 0:DV], ALU.mult, ALU.add).then_inc(dve_evac, 1)
                elif k == "intra":
                    need(dve, E_, mm, s.job + 1)
                    p = ptg[:, s.seq % 2, :]
                    link(dve.copy_predicated(p, mask_f[:, :], b_[:, 0:P]))
                    dve.copy_predicated(p, mask_b[:, :], b_[:, P:2 * P]).then_inc(dve_evac, 1)
                elif k == "o":
                    need(dve, E_, mm, s.job + 1)
                    dve.tensor_copy(o_gla[:, s.i, s.h * DV:(s.h + 1) * DV], b_[:, 0:DV]).then_inc(dve_evac, 1)
                elif k == "gstat":
                    need(dve, E_, gla_sq, NT * GH)
                    dve.tensor_scalar(grstd[:, :, :], gss[:, :, :], 1.0 / DV, EPS, ALU.mult, ALU.add).then_inc(gvar, 1)
                    need(dve, E_, gstd_done, 1)
                    link(dve.reciprocal(grstd[:, :, :], gstd[:, :, :]))
                    need(dve, E_, ggla_in, 16)
                elif k == "norm2":
                    i = s.i
                    need(dve, E_, sq2, i + 1)
                    dve.tensor_scalar(rstd[:, i:i + 1], ss[:, i:i + 1], 1.0 / D, EPS, ALU.mult, ALU.add).then_inc(var2, 1)
                    need(dve, E_, std2, i + 1)
                    link(dve.reciprocal(rstd[:, i:i + 1], std[:, i:i + 1]))
                    need(dve, E_, moe_in, 5 * 16)
                    dve.scalar_tensor_tensor(h2[:, i, :], x1[:, i, :], rstd[:, i:i + 1], g_moe[:, :],
                                             ALU.mult, ALU.mult).then_inc(h2_done, 1)
                elif k == "router":
                    need(dve, E_, mm, s.job + 1)
                    need(dve, E_, moe_in, 5 * 16)
                    i = s.i
                    if i == 0:
                        link(dve.memset(l_grp[:, :, :], -3e38))
                    mark(dve.tensor_tensor(l_grp[:, i, 0:NGRP], b_[:, 0:NGRP], r_bias[:, 0:NGRP], ALU.add))
                    dve.tensor_tensor(l_exp[:, i, :], b_[:, NGRP:NR], r_bias[:, NGRP:NR], ALU.add).then_inc(dve_evac, 1)
                elif k == "route":
                    settle()
                    need(dve, E_, dve_evac, jobs.evac[find(kind="router")[-1].job])
                    need(dve, E_, rconst, 1)
                    for i in range(NT):
                        mark(dve.max(top[:, i, :], l_grp[:, i, :]))
                    settle()
                    for i in range(NT):
                        mark(dve.max_index(top_at[:, i, :], top[:, i, :], l_grp[:, i, :]))
                    dve.tensor_tensor(ex[:, :, :], l_grp[:, :, :], top[:, :, 0:1].broadcast_to([P, NT, 8]),
                                      ALU.subtract).then_inc(route_neg, 1)
                    settle()
                    link(dve.tensor_copy(g_at[:, :], top_at[:, :, 0]))
                    lanes = lambda n: iota_row[:, 0:n].rearrange("p (o n) -> p o n", o=1).broadcast_to([P, NT, n])
                    link(dve.tensor_tensor(sel[:, :, :], lanes(NGRP), wide(g_at[:, :], NGRP), ALU.is_equal))
                    le = l_exp[:, :, :].rearrange("p i (g e) -> p i g e", e=EPG)
                    in_group = sel[:, :, :].rearrange("p i (g o) -> p i g o", o=1).broadcast_to([P, NT, NGRP, EPG])
                    link(dve.tensor_tensor(le, le, in_group, ALU.mult))
                    link(dve.tensor_scalar(sel[:, :, :], sel[:, :, :], -1.0, 3e38, ALU.add, ALU.mult))
                    link(dve.tensor_tensor(le, le, in_group, ALU.add))
                    for i in range(NT):
                        mark(dve.max(top2[:, i, :], l_exp[:, i, :]))
                    settle()
                    for i in range(NT):
                        mark(dve.max_index(top2_at[:, i, :], top2[:, i, :], l_exp[:, i, :]))
                    dve.tensor_tensor(ratio[:, :], top2[:, :, 1], top2[:, :, 0], ALU.subtract).then_inc(route_neg2, 1)
                    settle()
                    link(dve.tensor_copy(e_at[:, :, :], top2_at[:, :, 0:2]))
                    for j in range(2):
                        mark(dve.tensor_tensor(hot[j][:, :, :], lanes(NE), e_at[:, :, j:j + 1].broadcast_to([P, NT, NE]),
                                               ALU.is_equal))
                    settle()
                    mark(dve.memset(before[:, 0, :], 0.0))
                    link(dve.tensor_tensor(both[:, :, :], hot[0][:, :, :], hot[1][:, :, :], ALU.add))
                    for i in range(NT):
                        ins = dve.tensor_tensor(before[:, i + 1, :], before[:, i, :], both[:, i, :], ALU.add)
                        if i < NT - 1:
                            link(ins)
                    ins.then_inc(hot_done, 1)
                    need(dve, E_, route_exp, 1)
                    link(dve.tensor_reduce(p_grp[:, :], ex[:, :, :], AX.X, ALU.add))
                    link(dve.reciprocal(p_grp[:, :], p_grp[:, :]))
                    need(dve, E_, route_exp2, 1)
                    link(dve.tensor_scalar(g_at[:, :], ratio[:, :], 1.0, None, ALU.add))
                    link(dve.reciprocal(g_at[:, :], g_at[:, :]))
                    link(dve.tensor_tensor(pair_w[:, :, 0], g_at[:, :], p_grp[:, :], ALU.mult))
                    link(dve.tensor_tensor(pair_w[:, :, 1], pair_w[:, :, 0], ratio[:, :], ALU.mult))
                elif k == "rank":
                    need(dve, E_, mm, s.job + 1)
                    mark(dve.tensor_copy(rank[:, :, :], b_[:, 0:NT * NE].rearrange("p (i n) -> p i n", n=NE)))
                    dve.tensor_copy(tally[:, :], b_[:, NT * NE:(NT + 1) * NE]).then_inc(dve_evac, 1)
                elif k == "place":
                    settle()
                    need(dve, E_, dve_evac, jobs.evac[find(kind="rank")[0].job])
                    link(dve.tensor_scalar(n_over_e[:, :], tally[:, :], float(P), None, ALU.is_gt))
                    for m in range(2, T // P):
                        link(dve.scalar_tensor_tensor(n_over_e[:, :], tally[:, :], float(P * m), n_over_e[:, :],
                                                      ALU.is_gt, ALU.add))
                    link(dve.tensor_tensor_scan(over_end[:, :], ones[:, 0:NE], n_over_e[:, :], 0.0, ALU.mult, ALU.add))
                    link(dve.tensor_tensor(shift[:, :], over_end[:, :], n_over_e[:, :], ALU.subtract))
                    link(dve.tensor_tensor(shift[:, :], shift[:, :], iota_row[:, 0:NE], ALU.subtract))
                    link(dve.tensor_scalar(shift[:, :], shift[:, :], float(NE - 1), float(P), ALU.add, ALU.mult))
                    sh = shift[:, :].rearrange("p (o n) -> p o n", o=1).broadcast_to([P, NT, NE])
                    it = iota_row[:, 0:NE].rearrange("p (o n) -> p o n", o=1).broadcast_to([P, NT, NE])
                    link(dve.scalar_tensor_tensor(both[:, :, :], rank[:, :, :], float(P), sh, ALU.is_ge, ALU.mult))
                    link(dve.tensor_tensor(both[:, :, :], both[:, :, :], rank[:, :, :], ALU.add))
                    link(dve.scalar_tensor_tensor(both[:, :, :], it, float(P), both[:, :, :], ALU.mult, ALU.add))
                    for j in range(2):
                        link(dve.tensor_tensor(hot[j][:, :, :], hot[j][:, :, :], both[:, :, :], ALU.mult))
                        link(dve.tensor_reduce(pos[:, :, j], hot[j][:, :, :], AX.X, ALU.add))
                    link(dve.tensor_copy(pos_i[:, :, :], pos[:, :, :]))
                    mark(dve.tensor_copy(pair_idx[:, :, :], pos_i[:, :, :]))
                    link(dve.tensor_scalar(row_i[:, :, :], pos_i[:, :, :], P - 1, None, ALU.bitwise_and))
                    link(dve.tensor_copy(row_f[:, :, :], row_i[:, :, :]))
                    link(dve.tensor_tensor(slot_f[:, :, :], pos[:, :, :], row_f[:, :, :], ALU.subtract))
                    link(dve.tensor_scalar(slot_f[:, :, :], slot_f[:, :, :], 1.0 / P, None, ALU.mult))
                    need(dve, E_, h2_out, 16 * NT)
                    need(dve, E_, mm, find(kind="h2T")[-1].job + 1)
                    pairs = lambda x, n: x[:, :, :].rearrange("p i (j o) -> p (i j) o", o=1).broadcast_to([P, 2 * NT, n])
                    row = lambda n: iota_row[:, 0:n].rearrange("p (o n) -> p o n", o=1).broadcast_to([P, 2 * NT, n])
                    mark(dve.tensor_tensor(slot_is[:, :, :], row(EVEN), pairs(slot_f, EVEN), ALU.is_equal))
                    mark(dve.tensor_tensor(row_hot[:, :, :], row(P), pairs(row_f, P), ALU.is_equal))
                    settle()
                    both_of = lambda x: x[:, :, :].rearrange("p (i j) n -> p i (j n)", j=2)
                    dve.tensor_tensor(both_of(slot_hot), both_of(slot_is), wide(iota_tok[:, :], 2 * EVEN),
                                      ALU.mult).then_inc(place_done, 1)
                    link(dve.tensor_tensor(over_cmp[:, :, :],
                                           over_end[0:1, :].rearrange("p (o n) -> p o n", o=1).broadcast_to([1, OVER, NE]),
                                           iota_row[0:1, 0:OVER].rearrange("p (n o) -> p n o", o=1).broadcast_to([1, OVER, NE]),
                                           ALU.is_le))
                    link(dve.tensor_reduce(over_f[:, 0:OVER], over_cmp[:, :, :], AX.X, ALU.add))
                    link(dve.tensor_scalar(over_f[:, 0:OVER], over_f[:, 0:OVER], float(NE - 1), None, ALU.min))
                    link(dve.tensor_copy(over_f[:, OVER:OVER + 1], over_end[0:1, NE - 1:NE]))
                    dve.tensor_copy(over_row[:, :], over_f[:, :]).then_inc(over_done, 1)
                elif k == "table":
                    need(dve, E_, mm, s.job + 1)
                    link(dve.tensor_scalar(tab0[:, :], b_[:, 0:SLOTS], 0.0, float(SKIP), ALU.is_equal, ALU.mult))
                    link(dve.scalar_tensor_tensor(tab[:, :], b_[:, 0:SLOTS], -1.0, tab0[:, :], ALU.add, ALU.add))
                    dve.tensor_copy(slot_idx[:, :], tab[:, :]).then_inc(dve_evac, 1)

            def lo_weights(x, e, p, r):
                dve.wait_ge(w_hi_done[x], e + 1)
                dve.tensor_tensor(m_lo[x][:, r], m_raw[x][:, r], m_hi[x][:, p].bitcast(F32),
                                  ALU.subtract).then_inc(w_lo_done[x], 1)

            def lo_x(e, p):
                dve.wait_ge(xt_hi, e + 1)
                for half in range(2):
                    ins = dve.tensor_tensor(m_xT_lo[:, p, 4 * half:4 * half + 4, :],
                                            psum[B_XT[half]][:, :].rearrange("p (k t) -> p k t", t=P),
                                            m_xT_hi[:, p, 4 * half:4 * half + 4, :].bitcast(F32), ALU.subtract)
                ins.then_inc(xt_lo, 1)

            def gated(e, p, ring):
                dve.wait_ge(silu_done, e + 1)
                if not (isinstance(e, int) and e < ring):
                    dve.wait_ge(at_mm, e + (1 - ring))
                dve.tensor_tensor(m_a[:, p, :], m_sil[:, p, :], psum[B_GU[p]][:, FF:2 * FF], ALU.mult).then_inc(a_done, 1)

            def lo_a(e, p):
                dve.wait_ge(at_hi, e + 1)
                dve.tensor_tensor(m_aT_lo[:, p, :, :], psum[B_AT[p]][:, 0:2 * P].rearrange("p (k t) -> p k t", t=P),
                                  m_aT_hi[:, p, :, :].bitcast(F32), ALU.subtract).then_inc(at_lo, 1)

            def result(e, p, k):
                dve.wait_ge(y_mm, e + 1)
                if not (isinstance(k, int) and k == 0):
                    dve.wait_ge(y_out[p], k * 16)
                for half in range(2):
                    ins = dve.tensor_copy(m_y[:, p, half * 512:(half + 1) * 512], psum[B_Y[half]][:, :])
                ins.then_inc(y_done, 1)

            for x in ("up", "down"):
                dve.wait_ge(w_lo_done[x], 1)
                lo_weights(x, 1, 1, 1)
            lo_x(0, 0)
            lo_x(1, 1)

            def tile(e, p, k, r, u):
                gated(e, p, 2)
                if ahead(e, 2):
                    lo_weights("up", e + 2, p, later(r, u, 2)[0])
                lo_a(e, p)
                if ahead(e, 2):
                    lo_x(e + 2, p)
                if ahead(e, 1) and not first(e):
                    lo_weights("down", e + 1, 1 - p, later(r, u, 1)[0])
                result(e, p, k)

            first_tiles(dve.Fori, tile)

            def beyond_tile(e, j, k, u):
                for x in ("up", "down"):
                    lo_weights(x, e, 0, 0)
                lo_x(e, 0)
                gated(e, 0, 1)
                lo_a(e, 0)
                result(e, 0, k)

            beyond(dve, beyond_tile)
            for step in range(NT + 1):
                if step < NT:
                    i = step
                    dve.wait_ge(pair_in[i], 32)
                    for j in range(2):
                        ins = dve.scalar_tensor_tensor(x1[:, i, :], y_pair[:, i, j, :], pair_w[:, i, j:j + 1], x1[:, i, :],
                                                       ALU.mult, ALU.add)
                        if j == 0:
                            link(ins)
                    ins.then_inc(sum_done, 1)
                if step:
                    i = step - 1
                    dve.wait_ge(std3, i + 1)
                    link(dve.reciprocal(rstd[:, i:i + 1], std[:, i:i + 1]))
                    if i == 0:
                        dve.wait_ge(gfin_in, 16)
                    dve.scalar_tensor_tensor(y_fin[:, i, :], x1[:, i, :], rstd[:, i:i + 1], g_fin[:, :],
                                             ALU.mult, ALU.mult).then_inc(fin_done, 1)


def bucket_rows():
    import math
    import numpy as np

    half_buckets, max_exact = NBK // 2, NBK // 4
    out = np.zeros((NBK + 1, NV, VEC), np.float32)
    prompt, sample = (n for _, n in SEQS)
    for a, (win, dil, step) in enumerate(((128, 1, 1), (512, 4, prompt), (512, 4, sample),
                                          (2048, 16, prompt), (2048, 16, sample))):
        rel = np.arange(VEC) - (P - 1 + CH) if a == 0 else step * (np.arange(VEC) - (P - 1))
        n = np.abs(rel)
        large = max_exact + (np.log(np.maximum(n, 1) / max_exact) / math.log(1024 / max_exact)
                             * (half_buckets - max_exact)).astype(np.int64)
        bucket = (rel > 0) * half_buckets + np.where(n < max_exact, n, np.minimum(large, half_buckets - 1))
        ok = (rel % dil == 0) & (n <= win // 2)
        for x in range(VEC):
            if ok[x]:
                out[bucket[x], a, x] = 1.0
            else:
                out[NBK, a, x] = NEG
    return out.reshape(NBK + 1, NV * VEC)


INPUTS = ["x_prompt", "x_sample", "norm_mix", "w_in", "rel_bias", "w_gate_f", "b_gate_f", "w_gate_b", "b_gate_b",
          "gla_norm", "w_proj_a", "w_proj_b", "w_out", "norm_moe", "w_router_group", "b_router_group",
          "w_router_expert", "b_router_expert", "w_exp_gate", "w_exp_up", "w_exp_down", "norm_final"]


def kernel(**inputs):
    import numpy as np
    import concourse.bacc as bacc
    from concourse.bass_utils import run_bass_kernel_spmd

    nc = bacc.Bacc("TRN2", target_bir_lowering=False, num_devices=1)
    arrays = {name: np.ascontiguousarray(inputs[name]) for name in INPUTS}
    arrays["const_buckets"] = bucket_rows()
    A = {name: nc.dram_tensor(f"in_{name}", a.shape, mybir.dt.from_np(a.dtype), kind="ExternalInput").ap()
         for name, a in arrays.items()}
    outs = [nc.dram_tensor(f"y_{name}", (1, rows, D), F32, kind="ExternalOutput").ap()
            for name, rows in (("prompt", S_PROMPT), ("sample", S_SAMPLE))]
    build(nc, A, outs)
    r = run_bass_kernel_spmd(nc, [{f"in_{name}": a for name, a in arrays.items()}], core_ids=[0])
    return r.results[0]["y_prompt"], r.results[0]["y_sample"]
```
